# Optimizing a Trainium2 kernel written in Bass

```python
import jax, jax.numpy as jnp
from jax import lax
import numpy as np

D_MODEL = 1024
BATCH = 1
SEQ = 512
DEPTH = 2

N_MIXERS = 2
EPS = 1e-6
NEG_INF = -1e30
HG_HEADS = 8
HG_DK = 128
HG_DV = D_MODEL // HG_HEADS
HG_CHUNK = 64
NSA_HEADS = 16
NSA_KV = 4
NSA_GROUP = NSA_HEADS // NSA_KV
NSA_HD = D_MODEL // NSA_HEADS
CMP_LEN = 32
CMP_STRIDE = 16
SEL_LEN = 64
SEL_TOPK = 16
WINDOW = 512
Q_BLOCK = 32
FORCED_SCORE = 1e4
D_FF = 2816
CONV_W = 3


def rmsnorm(x, g):
    xf = x.astype(jnp.float32)
    y = xf * lax.rsqrt(jnp.mean(xf * xf, axis=-1, keepdims=True) + EPS)
    return (y * g).astype(x.dtype)

def alibi_slopes(n):
    return jnp.asarray([2.0 ** (-8.0 * (h + 1) / n) for h in range(n)], jnp.float32)

def hgrn2_mixer(h, w_in, w_out, g_norm, lb):
    B, S, _ = h.shape
    fd = HG_HEADS * HG_DK
    proj = h @ w_in
    q, f_pre, i_in, g = jnp.split(proj, [fd, 2 * fd, 2 * fd + D_MODEL], axis=-1)
    f_pre = f_pre.astype(jnp.float32)
    log_f = jnp.log(lb + (1.0 - lb) * jax.nn.sigmoid(f_pre))
    k = (1.0 - lb) * jax.nn.sigmoid(-f_pre)
    n = S // HG_CHUNK

    def chunks(t, d):
        return t.astype(jnp.float32).reshape(B, n, HG_CHUNK, HG_HEADS, d).transpose(1, 0, 3, 2, 4)

    xs = (chunks(q, HG_DK), chunks(k, HG_DK), chunks(i_in, HG_DV), chunks(log_f, HG_DK))
    causal = jnp.tril(jnp.ones((HG_CHUNK, HG_CHUNK), bool))[:, :, None]

    def step(state, inp):
        qc, kc, vc, lfc = inp
        b = jnp.cumsum(lfc, axis=2)
        o_inter = jnp.einsum('bhtk,bhkv->bhtv', qc * jnp.exp(b), state)
        diff = b[:, :, :, None, :] - b[:, :, None, :, :]
        decay = jnp.exp(jnp.where(causal, diff, NEG_INF))
        scores = jnp.einsum('bhtk,bhsk,bhtsk->bhts', qc, kc, decay)
        o_intra = jnp.einsum('bhts,bhsv->bhtv', scores, vc)
        b_last = b[:, :, -1:, :]
        state = state * jnp.exp(b_last[:, :, 0, :, None]) + jnp.einsum(
            'bhsk,bhsv->bhkv', kc * jnp.exp(b_last - b), vc)
        return state, o_inter + o_intra

    s0 = jnp.zeros((B, HG_HEADS, HG_DK, HG_DV), jnp.float32)
    _, o = lax.scan(step, s0, xs)
    o = o.transpose(1, 0, 3, 2, 4).reshape(B, S, HG_HEADS, HG_DV)
    o = rmsnorm(o, g_norm).reshape(B, S, D_MODEL)
    o = o * jax.nn.silu(g.astype(jnp.float32))
    return o.astype(h.dtype) @ w_out

def nsa_mixer(h, w_in, w_out, cmp_pe, cmp_w1, cmp_w2):
    B, S, _ = h.shape
    G, HPG, HD = NSA_KV, NSA_GROUP, NSA_HD
    nc = (S - CMP_LEN) // CMP_STRIDE + 1
    ns = S // SEL_LEN
    k_sel_n = min(SEL_TOPK, ns)
    kvd = G * HD
    split_at = [D_MODEL + j * kvd for j in range(7)]
    q, k_c, v_c, k_s, v_s, k_w, v_w, gate = jnp.split(h @ w_in, split_at, axis=-1)
    q = q.reshape(B, S, G, HPG, HD)
    gate = jax.nn.sigmoid(gate.astype(jnp.float32)).reshape(B, S, G, HPG, 3)

    def kv(t):
        return t.reshape(B, S, G, HD)

    cidx = (np.arange(nc) * CMP_STRIDE)[:, None] + np.arange(CMP_LEN)[None, :]

    def compress(t, pe, w1, w2):
        blocks = kv(t)[:, cidx] + pe[None, None, :, None, :]
        blocks = blocks.transpose(0, 1, 3, 2, 4).reshape(B, nc, G, CMP_LEN * HD)
        return jax.nn.silu(blocks @ w1) @ w2

    kc = compress(k_c, cmp_pe[0], cmp_w1[0], cmp_w2[0])
    vc = compress(v_c, cmp_pe[1], cmp_w1[1], cmp_w2[1])
    cmp_end = jnp.asarray(np.arange(nc) * CMP_STRIDE + CMP_LEN - 1, jnp.int32)
    cmp_mid = jnp.asarray(np.arange(nc) * CMP_STRIDE + (CMP_LEN - 1) / 2.0, jnp.float32)
    ci = np.arange(nc)[:, None] * CMP_STRIDE
    sj = np.arange(ns)[None, :] * SEL_LEN
    overlap = jnp.asarray((ci <= sj + SEL_LEN - 1) & (ci + CMP_LEN - 1 >= sj), jnp.float32)

    ks_blk = kv(k_s).reshape(B, ns, SEL_LEN, G, HD).transpose(0, 3, 1, 2, 4)
    vs_blk = kv(v_s).reshape(B, ns, SEL_LEN, G, HD).transpose(0, 3, 1, 2, 4)
    pad = ((0, 0), (WINDOW, 0), (0, 0), (0, 0))
    kw_pad = jnp.pad(kv(k_w), pad)
    vw_pad = jnp.pad(kv(v_w), pad)

    slopes = alibi_slopes(NSA_HEADS).reshape(G, HPG)
    scale = HD ** -0.5
    blk_ids = jnp.arange(ns)
    bi = jnp.arange(B)[:, None, None, None]
    gi = jnp.arange(G)[None, :, None, None]

    def block(i):
        q0 = i * Q_BLOCK
        t = q0 + jnp.arange(Q_BLOCK)
        qb = lax.dynamic_slice_in_dim(q, q0, Q_BLOCK, axis=1)
        gb = lax.dynamic_slice_in_dim(gate, q0, Q_BLOCK, axis=1)
        s_c = jnp.einsum('bqghd,bngd->bghqn', qb, kc, preferred_element_type=jnp.float32) * scale
        dist_c = t[:, None].astype(jnp.float32) - cmp_mid[None, :]
        s_c = s_c - slopes[None, :, :, None, None] * dist_c
        valid_c = cmp_end[None, :] <= t[:, None]
        p_c = jax.nn.softmax(jnp.where(valid_c, s_c, NEG_INF), axis=-1)
        p_c = p_c * (t >= CMP_LEN - 1).astype(jnp.float32)[None, None, None, :, None]
        o_c = jnp.einsum('bghqn,bngd->bqghd', p_c, vc)
        imp = jnp.einsum('bghqn,nj->bgqj', p_c, overlap)
        cur = t // SEL_LEN
        valid_s = blk_ids[None, :] * SEL_LEN <= t[:, None]
        forced = ((blk_ids[None, :] == 0) | (blk_ids[None, :] == cur[:, None])
                  | (blk_ids[None, :] == cur[:, None] - 1)) & valid_s
        score = jnp.where(forced, FORCED_SCORE, jnp.where(valid_s, imp, -1.0))
        _, idx = lax.top_k(score, k_sel_n)
        k_sel = ks_blk[bi, gi, idx]
        v_sel = vs_blk[bi, gi, idx].reshape(B, G, Q_BLOCK, k_sel_n * SEL_LEN, HD)
        pos = idx[..., None] * SEL_LEN + jnp.arange(SEL_LEN)
        s_s = jnp.einsum('bqghd,bgqkld->bghqkl', qb, k_sel, preferred_element_type=jnp.float32) * scale
        dist_s = (t[None, None, :, None, None] - pos).astype(jnp.float32)
        s_s = s_s - slopes[None, :, :, None, None, None] * dist_s[:, :, None]
        mask_s = (pos <= t[None, None, :, None, None])[:, :, None]
        s_s = jnp.where(mask_s, s_s, NEG_INF).reshape(B, G, HPG, Q_BLOCK, k_sel_n * SEL_LEN)
        o_s = jnp.einsum('bghqm,bgqmd->bqghd', jax.nn.softmax(s_s, axis=-1), v_sel)
        kw = lax.dynamic_slice_in_dim(kw_pad, q0, Q_BLOCK + WINDOW, axis=1)
        vw = lax.dynamic_slice_in_dim(vw_pad, q0, Q_BLOCK + WINDOW, axis=1)
        s_pos = q0 - WINDOW + jnp.arange(Q_BLOCK + WINDOW)
        s_w = jnp.einsum('bqghd,bsgd->bghqs', qb, kw, preferred_element_type=jnp.float32) * scale
        s_w = s_w - slopes[None, :, :, None, None] * (t[:, None] - s_pos[None, :]).astype(jnp.float32)
        mask_w = (s_pos[None, :] <= t[:, None]) & (s_pos[None, :] > t[:, None] - WINDOW) & (s_pos[None, :] >= 0)
        o_w = jnp.einsum('bghqs,bsgd->bqghd', jax.nn.softmax(jnp.where(mask_w, s_w, NEG_INF), axis=-1), vw)
        return gb[..., 0, None] * o_c + gb[..., 1, None] * o_s + gb[..., 2, None] * o_w

    o = lax.map(block, jnp.arange(S // Q_BLOCK))
    o = o.transpose(1, 0, 2, 3, 4, 5).reshape(B, S, D_MODEL)
    return o.astype(h.dtype) @ w_out

def conv_ffn(h, w_up, conv_w, conv_b, w_down):
    a, v = jnp.split(h @ w_up, 2, axis=-1)
    a = lax.conv_general_dilated(a, conv_w[:, None, :].astype(a.dtype), window_strides=(1,),
                                 padding=[(CONV_W - 1, 0)], dimension_numbers=('NWC', 'WIO', 'NWC'),
                                 feature_group_count=D_FF) + conv_b
    return (jax.nn.silu(a) * v) @ w_down

def first_inputs(seed: int = 0) -> dict:
    key = jax.random.key(seed)
    ks = jax.random.split(key, 24)
    n_a = (DEPTH + 1) // 2
    n_b = DEPTH // 2
    D = D_MODEL
    nsa_in = D + 6 * NSA_KV * NSA_HD + 3 * NSA_HEADS

    def nrm(k, shape, s):
        return jax.random.normal(k, shape, jnp.float32) * s

    return {
        'x': nrm(ks[0], (BATCH, SEQ, D), 1.0),
        'c': nrm(ks[1], (BATCH, D), 1.0),
        'ada_w': nrm(ks[2], (DEPTH, D, 6 * D), 0.5 * D ** -0.5),
        'ada_b': nrm(ks[3], (DEPTH, 6 * D), 0.02),
        'norm_mix': 1.0 + nrm(ks[4], (DEPTH, D), 0.02),
        'norm_ffn': 1.0 + nrm(ks[5], (DEPTH, D), 0.02),
        'final_norm': 1.0 + nrm(ks[6], (D,), 0.02),
        'hg_w_in': nrm(ks[7], (n_a, D, 2 * HG_HEADS * HG_DK + 2 * D), D ** -0.5),
        'hg_w_out': nrm(ks[8], (n_a, D, D), D ** -0.5),
        'hg_gnorm': 1.0 + nrm(ks[9], (n_a, HG_DV), 0.02),
        'hg_lb': nrm(ks[10], (n_a + 1, HG_HEADS * HG_DK), 0.5),
        'nsa_w_in': nrm(ks[11], (n_b, D, nsa_in), D ** -0.5),
        'nsa_w_out': nrm(ks[12], (n_b, D, D), D ** -0.5),
        'nsa_cmp_pe': nrm(ks[13], (n_b, 2, CMP_LEN, NSA_HD), 0.1),
        'nsa_cmp_w1': nrm(ks[14], (n_b, 2, CMP_LEN * NSA_HD, NSA_HD), (CMP_LEN * NSA_HD) ** -0.5),
        'nsa_cmp_w2': nrm(ks[15], (n_b, 2, NSA_HD, NSA_HD), NSA_HD ** -0.5),
        'ffn_w_up': nrm(ks[16], (DEPTH, D, 2 * D_FF), D ** -0.5),
        'ffn_conv_w': nrm(ks[17], (DEPTH, CONV_W, D_FF), CONV_W ** -0.5),
        'ffn_conv_b': nrm(ks[18], (DEPTH, D_FF), 0.02),
        'ffn_w_down': nrm(ks[19], (DEPTH, D_FF, D), D_FF ** -0.5),
    }

def first_block(x, c, ada_w, ada_b, norm_mix, norm_ffn, final_norm, hg_w_in, hg_w_out, hg_gnorm, hg_lb,
              nsa_w_in, nsa_w_out, nsa_cmp_pe, nsa_cmp_w1, nsa_cmp_w2, ffn_w_up, ffn_conv_w, ffn_conv_b,
              ffn_w_down):
    lb_all = jnp.cumsum(jax.nn.softmax(hg_lb.astype(jnp.float32), axis=0), axis=0)
    c_act = jax.nn.silu(c)
    for layer in range(DEPTH):
        mod = c_act @ ada_w[layer] + ada_b[layer]
        sh1, sc1, g1, sh2, sc2, g2 = [m[:, None, :] for m in jnp.split(mod, 6, axis=-1)]
        hmix = rmsnorm(x, norm_mix[layer]) * (1.0 + sc1) + sh1
        j = layer // N_MIXERS
        if layer % N_MIXERS == 0:
            y = hgrn2_mixer(hmix, hg_w_in[j], hg_w_out[j], hg_gnorm[j], lb_all[j])
        else:
            y = nsa_mixer(hmix, nsa_w_in[j], nsa_w_out[j], nsa_cmp_pe[j], nsa_cmp_w1[j], nsa_cmp_w2[j])
        x = x + g1 * y
        hffn = rmsnorm(x, norm_ffn[layer]) * (1.0 + sc2) + sh2
        x = x + g2 * conv_ffn(hffn, ffn_w_up[layer], ffn_conv_w[layer], ffn_conv_b[layer], ffn_w_down[layer])
    return rmsnorm(x, final_norm)


DEPTH_2 = 1

FFN_RES_WEIGHT = 0.5
CONV_DIM = D_MODEL
CONV_K = 3
GLA_HEADS = 4
GLA_DK = D_MODEL // 2 // GLA_HEADS
GLA_DV = D_MODEL // GLA_HEADS
GLA_QK = GLA_HEADS * GLA_DK
GLA_V = GLA_HEADS * GLA_DV
GATE_RANK = 16
GATE_TAU = 16.0
CHUNK = 64
IN_SIZES = (CONV_DIM, CONV_DIM, CONV_DIM, GLA_QK, GLA_QK, GLA_V, GATE_RANK, GLA_V, D_MODEL, D_MODEL)
IN_COLS = sum(IN_SIZES)
SPLIT_POINTS = tuple(int(s) for s in np.cumsum(IN_SIZES)[:-1])


def rmsnorm_2(x, g):
    xf = x.astype(jnp.float32)
    y = xf * lax.rsqrt(jnp.mean(xf * xf, axis=-1, keepdims=True) + EPS)
    return (y * g.astype(jnp.float32)).astype(x.dtype)

def swiglu(x, w_gu, w_down):
    g, u = jnp.split(x @ w_gu, 2, axis=-1)
    return (jax.nn.silu(g) * u) @ w_down

def causal_short_conv(u, w):
    S = u.shape[1]
    up = jnp.pad(u, ((0, 0), (CONV_K - 1, 0), (0, 0)))
    out = up[:, 0:S] * w[0]
    for j in range(1, CONV_K):
        out = out + up[:, j:j + S] * w[j]
    return out

def gla_chunked(q, k, v, log_a):
    B, S = q.shape[0], q.shape[1]
    N = S // CHUNK
    f32 = jnp.float32

    def to_chunks(t):
        return t.reshape(B, N, CHUNK, GLA_HEADS, t.shape[-1]).transpose(0, 3, 1, 2, 4).astype(f32)

    qc = to_chunks(q) * (GLA_DK ** -0.5)
    kc, vc, gc = to_chunks(k), to_chunks(v), to_chunks(log_a)
    b = jnp.cumsum(gc, axis=3)
    b_last = b[:, :, :, -1:]
    b_ref = b[:, :, :, CHUNK // 2 - 1:CHUNK // 2]

    q_ref = qc * jnp.exp(b - b_ref)
    k_ref = kc * jnp.exp(b_ref - b)
    scores = jnp.einsum('bhnid,bhnjd->bhnij', q_ref, k_ref)
    causal = jnp.tril(jnp.ones((CHUNK, CHUNK), dtype=bool))
    scores = jnp.where(causal, scores, 0.0)
    o_intra = jnp.einsum('bhnij,bhnjv->bhniv', scores, vc)

    q_inter = q_ref * jnp.exp(b_ref)
    k_state = kc * jnp.exp(b_last - b)
    kv = jnp.einsum('bhncd,bhncv->nbhdv', k_state, vc)
    decay = jnp.exp(b_last[:, :, :, 0]).transpose(2, 0, 1, 3)

    def step(state, inp):
        dec, kv_n = inp
        return state * dec[..., None] + kv_n, state

    init = jnp.zeros((B, GLA_HEADS, GLA_DK, GLA_DV), f32)
    _, states = lax.scan(step, init, (decay, kv))
    o_inter = jnp.einsum('bhncd,nbhdv->bhncv', q_inter, states)
    o = o_intra + o_inter
    return o.transpose(0, 2, 3, 1, 4).reshape(B, S, GLA_HEADS, GLA_DV)

def hybrid_mixer(h, w_in, conv_w, gate_w_up, gate_b, gla_norm_g, w_out_conv, w_out_gla, w_o):
    B, S, _ = h.shape
    z = h @ w_in
    cb, cc, cu, q, k, v, g_lr, r, ga, gb = jnp.split(z, SPLIT_POINTS, axis=-1)

    y_conv = (cb * causal_short_conv(cc * cu, conv_w)) @ w_out_conv

    log_a = jax.nn.log_sigmoid((g_lr @ gate_w_up + gate_b).astype(jnp.float32)) / GATE_TAU
    o = gla_chunked(q.reshape(B, S, GLA_HEADS, GLA_DK),
                    k.reshape(B, S, GLA_HEADS, GLA_DK),
                    v.reshape(B, S, GLA_HEADS, GLA_DV),
                    log_a.reshape(B, S, GLA_HEADS, GLA_DK))
    o = o * lax.rsqrt(jnp.mean(o * o, axis=-1, keepdims=True) + EPS)
    o = o.reshape(B, S, GLA_V) * gla_norm_g.astype(jnp.float32)
    y_gla = (o.astype(h.dtype) * jax.nn.silu(r)) @ w_out_gla

    merged = jax.nn.sigmoid(ga) * y_conv + jax.nn.sigmoid(gb) * y_gla
    return merged @ w_o

def second_inputs(seed: int = 0) -> dict:
    key = jax.random.key(seed)
    ks = jax.random.split(key, 20)
    f32 = jnp.float32

    def nrm(k, shape, fan_in):
        return jax.random.normal(k, shape, f32) * (fan_in ** -0.5)

    def gain(k, shape):
        return 1.0 + 0.02 * jax.random.normal(k, shape, f32)

    L = DEPTH_2
    return {
        'x': jax.random.normal(ks[0], (BATCH, SEQ, D_MODEL), f32),
        'norm_ffn1_g': gain(ks[1], (L, D_MODEL)),
        'ffn1_w_gu': nrm(ks[2], (L, D_MODEL, 2 * D_FF), D_MODEL),
        'ffn1_w_down': nrm(ks[3], (L, D_FF, D_MODEL), D_FF),
        'norm_mix_g': gain(ks[4], (L, D_MODEL)),
        'w_in': nrm(ks[5], (L, D_MODEL, IN_COLS), D_MODEL),
        'conv_w': nrm(ks[6], (L, CONV_K, CONV_DIM), CONV_K),
        'gate_w_up': nrm(ks[7], (L, GATE_RANK, GLA_QK), GATE_RANK),
        'gate_b': 0.1 * jax.random.normal(ks[8], (L, GLA_QK), f32),
        'gla_norm_g': gain(ks[9], (L, GLA_V)),
        'w_out_conv': nrm(ks[10], (L, CONV_DIM, D_MODEL), CONV_DIM),
        'w_out_gla': nrm(ks[11], (L, GLA_V, D_MODEL), GLA_V),
        'w_o': nrm(ks[12], (L, D_MODEL, D_MODEL), D_MODEL),
        'norm_ffn2_g': gain(ks[13], (L, D_MODEL)),
        'ffn2_w_gu': nrm(ks[14], (L, D_MODEL, 2 * D_FF), D_MODEL),
        'ffn2_w_down': nrm(ks[15], (L, D_FF, D_MODEL), D_FF),
        'final_norm_g': gain(ks[16], (D_MODEL,)),
    }

def second_block(x, norm_ffn1_g, ffn1_w_gu, ffn1_w_down, norm_mix_g, w_in, conv_w, gate_w_up, gate_b,
              gla_norm_g, w_out_conv, w_out_gla, w_o, norm_ffn2_g, ffn2_w_gu, ffn2_w_down, final_norm_g):
    for l in range(DEPTH_2):
        x = x + FFN_RES_WEIGHT * swiglu(rmsnorm_2(x, norm_ffn1_g[l]), ffn1_w_gu[l], ffn1_w_down[l])
        x = x + hybrid_mixer(rmsnorm_2(x, norm_mix_g[l]), w_in[l], conv_w[l], gate_w_up[l], gate_b[l],
                             gla_norm_g[l], w_out_conv[l], w_out_gla[l], w_o[l])
        x = x + FFN_RES_WEIGHT * swiglu(rmsnorm_2(x, norm_ffn2_g[l]), ffn2_w_gu[l], ffn2_w_down[l])
    return rmsnorm_2(x, final_norm_g)


def setup_inputs(seed=0):
    out = dict(first_inputs(seed))
    for name, value in second_inputs(seed + 1).items():
        if name != "x":
            out[name + "_2"] = value
    return out


def reference(
    x, c, ada_w, ada_b, norm_mix, norm_ffn, final_norm, hg_w_in, hg_w_out, hg_gnorm, hg_lb,
    nsa_w_in, nsa_w_out, nsa_cmp_pe, nsa_cmp_w1, nsa_cmp_w2, ffn_w_up, ffn_conv_w, ffn_conv_b,
    ffn_w_down, norm_ffn1_g_2, ffn1_w_gu_2, ffn1_w_down_2, norm_mix_g_2, w_in_2, conv_w_2,
    gate_w_up_2, gate_b_2, gla_norm_g_2, w_out_conv_2, w_out_gla_2, w_o_2, norm_ffn2_g_2,
    ffn2_w_gu_2, ffn2_w_down_2, final_norm_g_2,
):
    x = first_block(
        x, c, ada_w, ada_b, norm_mix, norm_ffn, final_norm, hg_w_in, hg_w_out, hg_gnorm, hg_lb,
        nsa_w_in, nsa_w_out, nsa_cmp_pe, nsa_cmp_w1, nsa_cmp_w2, ffn_w_up, ffn_conv_w,
        ffn_conv_b, ffn_w_down,
    )
    return second_block(
        x, norm_ffn1_g_2, ffn1_w_gu_2, ffn1_w_down_2, norm_mix_g_2, w_in_2, conv_w_2,
        gate_w_up_2, gate_b_2, gla_norm_g_2, w_out_conv_2, w_out_gla_2, w_o_2, norm_ffn2_g_2,
        ffn2_w_gu_2, ffn2_w_down_2, final_norm_g_2,
    )


_drawn_inputs = setup_inputs


def setup_inputs(seed=0):
    import zlib

    import numpy as np

    out = dict(_drawn_inputs(seed))
    spreads = {}
    factors = {'norm_mix': 4.277,
     'norm_ffn': 4.864,
     'hg_gnorm': 8.0,
     'nsa_cmp_pe': 4.323,
     'ffn_conv_b': 7.454,
     'norm_ffn1_g_2': 5.104,
     'norm_mix_g_2': 2.9,
     'gate_b_2': 4.664,
     'gla_norm_g_2': 96.659,
     'norm_ffn2_g_2': 36.008,
     'final_norm_g_2': 20.286}
    for name, (base, spread) in spreads.items():
        noise = np.random.default_rng([zlib.crc32(name.encode()), seed]).standard_normal(out[name].shape)
        drawn = base * np.exp(spread * noise) if base else spread * noise
        out[name] = __import__('jax').numpy.asarray(drawn.astype(out[name].dtype))
    for name, factor in factors.items():
        out[name] = (out[name] * factor).astype(out[name].dtype)
    return out
```

```python
import numpy as np
import concourse.bass as bass
from concourse import mybir
from contextlib import ExitStack

ALU = mybir.AluOpType
ACT = mybir.ActivationFunctionType
F32 = mybir.dt.float32
F32R = mybir.dt.float32r
U32 = mybir.dt.uint32
AX = mybir.AxisListType

P = 128
T = 512
D = 1024
KT = D // P
FF = 2816
FT = FF // P
UNIT = 1024
RAW_SLOTS = 5
SPLIT_SLOTS = 4
AHEAD = 2
EPS = 1e-6
CHUNK = 64
NCHUNK = T // CHUNK
NSA_HEADS, NSA_GROUPS, HD = 16, 4, 64
CMP_LEN, CMP_STRIDE = 32, 16
NCMP = (T - CMP_LEN) // CMP_STRIDE + 1
MASKED = 1e30

COLS = {}


def _columns():
    at = 0
    for name, n in (("c", 8), ("norm_mix0", 8), ("norm_ffn0", 8), ("norm_mix1", 8), ("norm_ffn1", 8),
                    ("final_norm", 8), ("b_norm_ffn1", 8), ("b_norm_mix", 8), ("b_norm_ffn2", 8),
                    ("b_final_norm", 8), ("ada_b", 96), ("gnorm", 1), ("hg_lb", 16),
                    ("conv_w0", 66), ("conv_b0", 22), ("conv_w1", 66), ("conv_b1", 22),
                    ("b_conv_w", 24), ("gate_b", 4), ("gla_norm", 8), ("pe", 64)):
        COLS[name] = (at, n)
        at += n
    return at


NCOLS = _columns()


class Lane:

    def __init__(self, name, sem):
        self.name, self.sem, self.count, self.steps, self.met = name, sem, 0, [], {}

    def do(self, fn, after=(), signal=True, dma_sem=None):
        waits = {}
        for token in after:
            if token is None:
                continue
            sem, value = token
            if value > self.met.get(sem.name, 0):
                self.met[sem.name] = value
                waits[sem.name] = (sem, value)
        if dma_sem is not None:
            self.steps.append((list(waits.values()), fn, dma_sem, 16))
            return None
        self.steps.append((list(waits.values()), fn, self.sem if signal else None, 1))
        if signal:
            self.count += 1
        return (self.sem, self.count)

    @property
    def last(self):
        return (self.sem, self.count) if self.count else None

    def emit(self, eng):
        for waits, fn, sem, n in self.steps:
            for s, v in waits:
                eng.wait_ge(s, v)
            ins = fn(eng)
            if sem is not None:
                ins.then_inc(sem, n)

    def tt(self, out, a, b, op, after=()):
        return self.do(lambda e: e.tensor_tensor(out, a, b, op), after)

    def ts(self, out, a, s1, s2, op0, op1=None, after=()):
        if op1 is None:
            return self.do(lambda e: e.tensor_scalar(out, a, s1, None, op0), after)
        return self.do(lambda e: e.tensor_scalar(out, a, s1, s2, op0, op1), after)

    def stt(self, out, a, s, b, op0, op1, after=()):
        return self.do(lambda e: e.scalar_tensor_tensor(out=out, in0=a, scalar=s, in1=b, op0=op0, op1=op1), after)

    def copy(self, out, a, after=()):
        return self.do(lambda e: e.tensor_copy(out, a), after)

    def memset(self, out, v, after=()):
        return self.do(lambda e: e.memset(out, v), after)

    def act(self, out, a, f, after=(), **kw):
        return self.do(lambda e: e.activation(out, a, f, **kw), after)

    def mm(self, out, lhsT, rhs, start, stop, after=(), signal=False):
        return self.do(lambda e: e.matmul(out, lhsT, rhs, start=start, stop=stop), after, signal)

    def tr(self, out, a, ident, after=(), signal=False):
        return self.do(lambda e: e.transpose(out, a, ident), after, signal)


class Slot:

    def __init__(self, buf, free=()):
        self.buf, self.free = buf, list(free)


class Ring:
    def __init__(self, bufs, free=()):
        self.slots, self.at = [Slot(b, free) for b in bufs], 0

    def next(self):
        s = self.slots[self.at % len(self.slots)]
        self.at += 1
        return s


def stream_plan():
    ada = [[("a", "ada", (l, g, kp), UNIT) for g in range(12) for kp in range(4)] for l in range(2)]
    plan = ada[0][:16]

    def fm(name, tiles):
        return [("w", name, (n,), UNIT) for n in tiles]

    def mix(main, extra):
        out, e = [], 0
        for i, u in enumerate(main):
            out.append(u)
            want = (i + 1) * len(extra) // len(main)
            out += extra[e:want]
            e = want
        return out

    def tm(name, groups):
        return [("w", name, (g, kp), UNIT) for g in groups for kp in range(4)]

    def down(name):
        return [("w", name, (n, k0), min(8, FT - k0) * P) for n in range(KT) for k0 in range(0, FT, 8)]

    def up(name):
        return fm(name, [t for j in range(FT) for t in (j, FT + j)])

    plan += mix(tm("hg_v", range(2)) + fm("hg_f", range(8)), ada[0][16:])
    plan += fm("hg_q", range(8)) + fm("hg_g", range(8)) + fm("hg_out", range(8))
    plan += mix(up("up0") + down("down0"), ada[1])
    plan += tm("nsa_v", range(1)) + [("w", "nsa_gate", (0,), 8 * 48)]
    plan += fm("nsa_kv", range(8)) + fm("nsa_q", range(8)) + fm("nsa_out", range(8))
    plan += up("up1") + down("down1")
    plan += up("bup1") + down("bdown1")
    plan += fm("b_conv", [8 * s + i for i in range(8) for s in (1, 2, 0)])
    for i in range(8):
        plan += fm("b_ga", [i]) + fm("b_out_conv", [i])
    plan += fm("b_glr", [0]) + tm("b_v", range(2))
    for h in range(4):
        plan += fm("b_q", [h]) + fm("b_k", [h])
    plan += fm("b_r", range(8))
    for i in range(8):
        plan += fm("b_gb", [i]) + fm("b_out_gla", [i])
    plan += fm("b_o", range(8)) + up("bup2") + down("bdown2")
    return plan


def build(nc, dram):
    plan = stream_plan()
    with ExitStack() as ctx:
        def sem(name):
            return ctx.enter_context(nc.semaphore(name))

        PE, DVE, SC, GP, SP = (Lane(n, sem(f"{n}_done")) for n in ("pe", "dve", "act", "pool", "sp"))
        raw_landed = [sem(f"raw_landed{i}") for i in range(RAW_SLOTS)]
        x_landed, cols_landed, cmp_landed, gup_landed = (sem(n) for n in ("x_landed", "cols_landed", "cmp_landed", "gup_landed"))
        out_stored = sem("out_stored")

        top = [(nc.sbuf_base + 31) // 32 * 32]

        def perm(name, shape, dt):
            size = int(np.prod(shape[1:])) * 4
            t = nc.alloc_sbuf_tensor_at(name, shape, dt, offset=top[0])
            top[0] += (size + 31) // 32 * 32
            return t

        x = perm("x", [P, KT, T], F32)
        h_at = top[0]
        h_hi = perm("h_hi", [P, KT, T], F32R)
        h_lo = perm("h_lo", [P, KT, T], F32R)
        hh32 = nc.alloc_sbuf_tensor_at("h_hi_f32", [P, KT, T], F32, offset=h_at)
        hl32 = nc.alloc_sbuf_tensor_at("h_lo_f32", [P, KT, T], F32, offset=h_at + KT * T * 4)
        raw = [perm(f"raw{i}", [P, UNIT], F32) for i in range(RAW_SLOTS)]
        w_hi = [perm(f"w_hi{i}", [P, UNIT], F32R) for i in range(SPLIT_SLOTS)]
        w_lo = [perm(f"w_lo{i}", [P, UNIT], F32R) for i in range(SPLIT_SLOTS)]
        ada_acc = [perm(f"ada_acc{i}", [P, T], F32) for i in range(2)]
        cols = perm("cols", [P, NCOLS + 1], F32)
        mod = perm("mod", [P, 2, 48], F32)
        gain = perm("gain", [P, KT], F32)
        ones = perm("ones", [P, P], F32)
        mean_d = perm("mean_d", [P, P], F32)
        ident = perm("ident", [P, P], F32)
        c_act = perm("c_act", [P, KT], F32)
        eps = cols[:, NCOLS:NCOLS + 1]
        lb = perm("lb", [P, 8], F32)
        one_m_lb = perm("one_m_lb", [P, 8], F32)
        arena = top[0]
        ends = [arena]

        def at(name, offset, shape, dt=F32):
            size = int(np.prod(shape[1:])) * 4
            ends.append(arena + offset + size)
            return nc.alloc_sbuf_tensor_at(name, shape, dt, offset=arena + offset)

        KB = 1024
        psum = [ctx.enter_context(nc.psum_tensor(f"bank{i}", [P, T], F32)) for i in range(8)]
        G = Ring([psum[i][:, :] for i in range(4)])
        S = Ring([psum[i][:, :] for i in range(4, 7)])
        O = Ring([psum[7][:, :]])

        def col(name, i=0, n=1):
            a, _ = COLS[name]
            return cols[:, a + i:a + i + n]

        class Stream:
            def __init__(self):
                self.read = 0
                self.seen = 0
                self.taken = 0
                self.raw_free = [[] for _ in range(RAW_SLOTS)]
                self.split_free = [[] for _ in range(SPLIT_SLOTS)]
                self.n_split = 0
                self.ready = []
                self.sums = []
                self.acc_free = [[], []]
                self.n_groups = 0
                self.mod_token = {}

            def load(self):
                while self.read < len(plan) and self.read < self.seen + RAW_SLOTS:
                    kind, name, index, n = plan[self.read]
                    s = self.read % RAW_SLOTS
                    src = dram[name][index[0]] if len(index) == 1 else (
                        dram[name][index[0], index[1], index[2]] if len(index) == 3 else None)
                    if src is None:
                        if name.startswith(("down", "bdown")):
                            src = dram[name][index[0], :, index[1] * P:index[1] * P + n]
                        else:
                            src = dram[name][index[0], index[1]]
                    dst = raw[s][:, 0:n]
                    SP.do(lambda e, dst=dst, src=src: e.dma_start(dst, src), self.raw_free[s], dma_sem=raw_landed[s])
                    self.read += 1

            def step(self):
                u = self.seen
                kind, name, index, n = plan[u]
                s = u % RAW_SLOTS
                landed = (raw_landed[s], 16 * (u // RAW_SLOTS + 1))
                src = raw[s][:, 0:n]
                if kind == "w":
                    q = self.n_split % SPLIT_SLOTS
                    hi, lo = w_hi[q][:, 0:n], w_lo[q][:, 0:n]
                    t_hi = SC.act(hi, src, ACT.Copy, after=[landed, *self.split_free[q]])
                    t_lo = DVE.tt(lo, src, hi.bitcast(F32), ALU.subtract, after=[landed, t_hi])
                    self.raw_free[s] = [t_hi, t_lo]
                    self.ready.append((name, index, hi, lo, t_lo, q))
                    self.n_split += 1
                else:
                    l, g, kp = index
                    if kp == 0:
                        self.fold(keep=1)
                    a = self.n_groups % 2
                    acc = ada_acc[a]
                    for j in range(2):
                        k = 2 * kp + j
                        w = src[:, j * T:(j + 1) * T]
                        if k == 0:
                            t = DVE.ts(acc[:, :], w, c_act[:, 0:1], None, ALU.mult,
                                       after=[landed, self.c_token, *self.acc_free[a]])
                        else:
                            t = DVE.stt(acc[:, :], w, c_act[:, k:k + 1], acc[:, :], ALU.mult, ALU.add,
                                        after=[landed, self.acc_token])
                        self.acc_token = t
                    self.raw_free[s] = [t]
                    if kp == 3:
                        self.sums.append((l, g, a, t))
                        self.n_groups += 1
                self.seen += 1
                self.load()

            def fold(self, keep=0):
                while len(self.sums) > keep:
                    l, g, a, t = self.sums.pop(0)
                    bank = S.next()
                    for i in range(4):
                        m = PE.mm(bank.buf[:, i:i + 1], ada_acc[a][:, i * P:(i + 1) * P], ones[:, 0:1], True, True,
                                  after=[t, ones_token, *bank.free], signal=(i == 3))
                    v = DVE.tt(mod[:, l, 4 * g:4 * g + 4], bank.buf[:, 0:4], col("ada_b", 48 * l + 4 * g, 4), ALU.add,
                               after=[m, cols_token])
                    self.acc_free[a] = [m]
                    bank.free = [v]
                    self.mod_token[l] = v

            def take(self, name, *index):
                while self.n_split < min(self.taken + 1 + AHEAD, n_w):
                    self.step()
                got = self.ready.pop(0)
                assert (got[0], got[1]) == (name, index), (got[0], got[1], name, index)
                self.taken += 1
                return got

            def done(self, unit, token):
                self.split_free[unit[5]] = [token]

        n_w = sum(p[0] == "w" for p in plan)
        stream = Stream()

        SP.do(lambda e: e.dma_start(cols[:, 0:NCOLS], dram["cols"]), dma_sem=cols_landed)
        cols_token = (cols_landed, 16)
        stream.load()
        SP.do(lambda e: e.dma_start(x[:, :, :], dram["x"]), dma_sem=x_landed)
        x_token = (x_landed, 16)
        GP.memset(mean_d[:, :], 1.0 / D)
        GP.memset(eps, EPS)
        GP.memset(ident[:, :], 0.0)
        ones_token = GP.memset(ones[:, :], 1.0)
        ident_token = GP.do(lambda e: e.affine_select(out=ident[:, :], in_=ident[:, :], compare_op=ALU.not_equal,
                                                      fill=1.0, base=0, pattern=[[-1, P]], channel_multiplier=1),
                            after=[ones_token])
        stream.c_token = SC.act(c_act[:, :], col("c", 0, 8), ACT.Silu, after=[cols_token])
        t = DVE.tt(lb[:, :], col("hg_lb", 0, 8), col("hg_lb", 8, 8), ALU.subtract, after=[cols_token])
        t = SC.act(lb[:, :], lb[:, :], ACT.Sigmoid, after=[t])
        lb_token = DVE.ts(one_m_lb[:, :], lb[:, :], -1.0, 1.0, ALU.mult, ALU.add, after=[t])

        x_ready = [x_token] * KT
        h_ready = [None] * KT
        h_dead = [None]

        def barrier():
            return [lane.last for lane in (PE, DVE, SC, GP)]

        def fm_product(name, *index, src_hi=None, src_lo=None, ready=None, bank=None, k0=0, nk=KT, first=True, last=True):
            src_hi, src_lo, ready = (src_hi or h_hi), (src_lo or h_lo), (ready or h_ready)
            unit = stream.take(name, *index)
            _, _, hi, lo, split, _ = unit
            bank = bank or G.next()
            for i in range(nk):
                k = k0 + i
                w = slice(i * P, (i + 1) * P)
                PE.mm(bank.buf, hi[:, w], src_hi[:, k, :], first and i == 0, False,
                      after=[split, ready[k], *(bank.free if first and i == 0 else [])])
                PE.mm(bank.buf, hi[:, w], src_lo[:, k, :], False, False)
                t = PE.mm(bank.buf, lo[:, w], src_hi[:, k, :], False, last and i == nk - 1, signal=(i == nk - 1))
            stream.done(unit, t)
            if src_hi is h_hi:
                h_dead[0] = t
            stream.fold()
            return bank, t

        def tm_product(name, group, evacuate):
            banks = [G.next() for _ in range(4)]
            for kp in range(4):
                unit = stream.take(name, group, kp)
                _, _, hi, lo, split, _ = unit
                for tok in range(4):
                    bank = banks[tok]
                    c = slice(tok * P, (tok + 1) * P)
                    for j in range(2):
                        k = 2 * kp + j
                        w = slice(j * T, (j + 1) * T)
                        PE.mm(bank.buf, h_hi[:, k, c], hi[:, w], k == 0, False,
                              after=[split, h_ready[k], *(bank.free if k == 0 else [])])
                        PE.mm(bank.buf, h_hi[:, k, c], lo[:, w], False, False)
                        t = PE.mm(bank.buf, h_lo[:, k, c], hi[:, w], False, k == KT - 1,
                                  signal=(j == 1 and (kp == 3 or tok == 3)))
                    if kp == 3:
                        evacuate(tok, bank, t)
                stream.done(unit, t)
                h_dead[0] = t
                stream.fold()

        def split_into(hi, lo, k, value, after, readers_done=()):
            t_hi = SC.act(hi[:, k, :], value, ACT.Copy, after=[*after, *readers_done])
            t_lo = DVE.tt(lo[:, k, :], value, hi[:, k, :].bitcast(F32), ALU.subtract, after=[*after, t_hi])
            return t_hi, t_lo

        sq_ring = Ring([hh32[:, 6, :], hh32[:, 7, :]])
        ssum = hh32[:, 5, :]
        rstd = hl32[:, 7, :]
        norm_state = {}

        def square_sum(k):
            slot = sq_ring.next()
            if k < 2:
                slot.free = [h_dead[0], DVE.last]
            t = SC.act(slot.buf, x[:, k, :], ACT.Square, after=[x_ready[k], *slot.free])
            if k == KT - 1:
                norm_state["last"] = (slot, t)
                return
            if k == 0:
                t = GP.ts(ssum, slot.buf, 1.0, None, ALU.mult, after=[t, h_dead[0], DVE.last])
            else:
                t = GP.tt(ssum, ssum, slot.buf, ALU.add, after=[t, norm_state["sum"]])
            norm_state["sum"] = t
            slot.free = [t]

        def inverse_rms(out, bank, n_token, after=()):
            t = SC.act(out, bank.buf, ACT.Ln, bias=eps[:, 0:1], after=[n_token, ones_token, *after])
            bank.free = [t]
            return SC.act(out, out, ACT.Exp, scale=-0.5, after=[t])

        def finish_rms():
            slot, t_last = norm_state["last"]
            bank = S.next()
            PE.mm(bank.buf, mean_d[:, :], ssum, True, False, after=[norm_state["sum"], ones_token, *bank.free])
            t = PE.mm(bank.buf, mean_d[:, :], slot.buf, False, True, after=[t_last], signal=True)
            return inverse_rms(rstd, bank, t, after=[h_dead[0]])

        def norm_to_h(gain_name, layer=None, which=0):
            t_r = finish_rms()
            if layer is None:
                g, shift, t_g = col(gain_name, 0, 8), None, cols_token
            else:
                t_g = DVE.stt(gain[:, :], mod[:, layer, 24 * which + 8:24 * which + 16], 1.0, col(gain_name, 0, 8),
                              ALU.add, ALU.mult, after=[stream.mod_token[layer], cols_token, DVE.last])
                g, shift = gain, mod[:, layer, 24 * which:24 * which + 8]
            for k in range(KT):
                v = hl32[:, k, :]
                t = DVE.stt(v, x[:, k, :], g[:, k:k + 1], rstd, ALU.mult, ALU.mult,
                            after=[t_r, t_g, x_ready[k], h_dead[0]])
                if shift is None:
                    t_hi = SC.act(h_hi[:, k, :], v, ACT.Copy, after=[t])
                    t = DVE.tt(h_lo[:, k, :], v, h_hi[:, k, :].bitcast(F32), ALU.subtract, after=[t_hi, t])
                else:
                    t_hi = SC.act(h_hi[:, k, :], v, ACT.Identity, bias=shift[:, k:k + 1], after=[t])
                    t = DVE.stt(h_lo[:, k, :], v, shift[:, k:k + 1], h_hi[:, k, :].bitcast(F32), ALU.add, ALU.subtract,
                                after=[t_hi, t])
                h_ready[k] = t

        def residual(k, bank, token, scale, after=()):
            x_ready[k] = DVE.stt(x[:, k, :], bank.buf, scale, x[:, k, :], ALU.mult, ALU.add,
                                 after=[token, x_ready[k], *after])
            bank.free = [x_ready[k]]
            square_sum(k)

        def normalize_x(gain_name):
            t_r = finish_rms()
            for k in range(KT):
                x_ready[k] = DVE.stt(x[:, k, :], x[:, k, :], col(gain_name, k), rstd, ALU.mult, ALU.mult,
                                     after=[t_r, x_ready[k], cols_token])

        def causal_conv(out, source, w, after, bias=None, free=()):
            if bias is None:
                t = DVE.ts(out, source, w[2], None, ALU.mult, after=[*after, *free])
            else:
                t = DVE.ts(out, source, w[2], bias, ALU.mult, ALU.add, after=[*after, *free])
            t = DVE.stt(out[:, 1:T], source[:, 0:T - 1], w[1], out[:, 1:T], ALU.mult, ALU.add, after=[t])
            return DVE.stt(out[:, 2:T], source[:, 0:T - 2], w[0], out[:, 2:T], ALU.mult, ALU.add, after=[t])

        phase = [0]

        def ffn(up, down, scale, conv=None):
            phase[0] += 1
            start = barrier()
            mid_hi = at(f"mid_hi{phase[0]}", 0, [P, FT, T], F32R)
            mid_lo = at(f"mid_lo{phase[0]}", 44 * KB, [P, FT, T], F32R)
            temps = Ring([at(f"act{phase[0]}_{i}", (88 + 2 * i) * KB, [P, T])[:, :] for i in range(3)], start)
            mid_ready = [None] * FT
            for j in range(FT):
                a, t_a = fm_product(up, j)
                v, t_v = fm_product(up, FT + j)
                s = temps.next()
                if conv is not None:
                    wn, bn = conv
                    t = causal_conv(s.buf, a.buf, [col(wn, 22 * i + j) for i in range(3)], [t_a, cols_token],
                                    bias=col(bn, j), free=s.free)
                    a.free = [t]
                    t = SC.act(s.buf, s.buf, ACT.Silu, after=[t])
                else:
                    t = SC.act(s.buf, a.buf, ACT.Silu, after=[t_a, *s.free])
                    a.free = [t]
                t = DVE.tt(s.buf, s.buf, v.buf, ALU.mult, after=[t, t_v])
                v.free = [t]
                t_hi, t_lo = split_into(mid_hi, mid_lo, j, s.buf, [t], start if j == 0 else ())
                s.free = [t_hi, t_lo]
                mid_ready[j] = t_lo
            for n in range(KT):
                bank = G.next()
                for k0 in range(0, FT, 8):
                    nk = min(8, FT - k0)
                    _, t = fm_product(down, n, k0, src_hi=mid_hi, src_lo=mid_lo, ready=mid_ready, bank=bank,
                                      k0=k0, nk=nk, first=(k0 == 0), last=(k0 + nk == FT))
                residual(n, bank, t, scale(n))

        class Gated:

            def __init__(self, tag, base, dv, block, start):
                self.dv, self.block, self.nb, self.start = dv, block, CHUNK // block, start
                o = [base]

                def take(name, shape, dt=F32):
                    size = int(np.prod(shape[1:])) * 4
                    t = at(f"{tag}_{name}", o[0], shape, dt)
                    o[0] += (size + 31) // 32 * 32
                    return t

                nb = self.nb
                self.kd = Ring([take(f"kd{i}", [P, NCHUNK, nb, CHUNK]) for i in range(2)], start)
                self.qd = Ring([take(f"qd{i}", [P, T]) for i in range(2)], start)
                self.qi = Ring([take(f"qi{i}", [P, T]) for i in range(2)], start)
                self.dec = Ring([take(f"dec{i}", [P, NCHUNK]) for i in range(2)], start)
                self.ks = Ring([take(f"ks{i}", [P, T]) for i in range(2)], start)
                self.kst = Ring([take("kst", [P, 4, P])], start)
                self.st = Ring([take("st", [P, NCHUNK, dv])], start)
                self.sc = Ring([take(f"sc{i}", [P, 4, P]) for i in range(2 if dv == P else 1)], start)
                self.sq = Ring([take(f"sq{i}", [P, T]) for i in range(2)], start)
                self.rstd = Ring([take("rstd", [P, T])], start)
                self.mask = take("mask", [P, 4 * CHUNK], U32)
                self.mean = take("mean", [P, P])
                self.one_reset = take("reset", [P, T])
                self.end = o[0]
                t0 = GP.memset(self.mean[:, :], 1.0 / dv, after=start)
                m = self.mask[:, :]
                mf = self.sc.slots[0].buf[:, :, 0:CHUNK]
                t = GP.memset(mf, 1.0, after=start)
                for half in range(2):
                    v = mf[64 * half:64 * half + 64, :, :]
                    t = GP.do(lambda e, v=v: e.affine_select(out=v, in_=v, compare_op=ALU.is_ge, fill=0.0, base=0,
                                                             pattern=[[0, 4], [1, CHUNK]], channel_multiplier=-1),
                              after=[t])
                t = DVE.copy(m.rearrange("p (c t) -> p c t", t=CHUNK), mf, after=[t])
                for s in self.sc.slots:
                    s.free = [GP.memset(s.buf[:, :, :], 0.0, after=[t, *start])]
                t = GP.memset(self.one_reset[:, :], 1.0, after=start)
                r = self.one_reset[:, :].rearrange("p (c s) -> p c s", s=CHUNK)
                self.const = GP.memset(r[:, :, 0:1], 0.0, after=[t])

            def running_sum(self, out, logs, after):
                return DVE.do(lambda e: e.tensor_tensor_scan(out, self.one_reset[:, :], logs, 0.0, ALU.mult, ALU.add),
                              after=[self.const, *after])

            def factors(self, q, t_q, k, t_k, b, t_b):
                bs, nb = self.block, self.nb
                kd, qd, qi, dec, ks = (r.next() for r in (self.kd, self.qd, self.qi, self.dec, self.ks))
                blocks = b.rearrange("p (n s) -> p n s", s=bs)
                ref = blocks[:, :, bs // 2 - 1:bs // 2]
                v = qd.buf[:, :].rearrange("p (n s) -> p n s", s=bs)
                t = DVE.tt(v, blocks, ref.to_broadcast([P, T // bs, bs]), ALU.subtract, after=[t_b, *qd.free])
                t = SC.act(qd.buf[:, :], qd.buf[:, :], ACT.Exp, after=[t])
                t_qd = DVE.tt(qd.buf[:, :], qd.buf[:, :], q, ALU.mult, after=[t, t_q])
                chunks = b.rearrange("p (c s) -> p c s", s=CHUNK)
                for_blocks = b.rearrange("p (c j s) -> p c j s", j=nb, s=bs)[:, :, :, bs // 2 - 1:bs // 2]
                kv4 = kd.buf[:, :, :, :]
                t = DVE.tt(kv4, for_blocks.to_broadcast([P, NCHUNK, nb, CHUNK]),
                           chunks.unsqueeze(2).to_broadcast([P, NCHUNK, nb, CHUNK]), ALU.subtract,
                           after=[t_b, *kd.free])
                flat = kd.buf[:, :, :, :].rearrange("p c j s -> p (c j s)")
                if nb > 1:
                    t = GP.do(lambda e: e.affine_select(out=kv4, in_=kv4, compare_op=ALU.is_ge, fill=-1.0e4,
                                                        base=bs - 1, pattern=[[0, NCHUNK], [bs, nb], [-1, CHUNK]],
                                                        channel_multiplier=0), [t])
                t = SC.act(flat, flat, ACT.Exp, after=[t])
                k4 = k.rearrange("p (c s) -> p c s", s=CHUNK).unsqueeze(2).to_broadcast([P, NCHUNK, nb, CHUNK])
                t_kd = DVE.tt(kv4, kv4, k4, ALU.mult, after=[t, t_k])
                t = SC.act(qi.buf[:, :], b, ACT.Exp, after=[t_b, *qi.free])
                ends_ = qi.buf[:, :].rearrange("p (c s) -> p c s", s=CHUNK)[:, :, CHUNK - 1:CHUNK]
                t_dec = DVE.copy(dec.buf[:, :].unsqueeze(2), ends_, after=[t, *dec.free])
                t_qi = GP.tt(qi.buf[:, :], qi.buf[:, :], q, ALU.mult, after=[t, t_q, t_dec])
                v = ks.buf[:, :].rearrange("p (c s) -> p c s", s=CHUNK)
                t = GP.tt(v, chunks[:, :, CHUNK - 1:CHUNK].to_broadcast([P, NCHUNK, CHUNK]), chunks, ALU.subtract,
                          after=[t_b, *ks.free])
                t_b_read = t
                t = SC.act(ks.buf[:, :], ks.buf[:, :], ACT.Exp, after=[t])
                t_ks = GP.tt(ks.buf[:, :], ks.buf[:, :], k, ALU.mult, after=[t, t_k])
                self.inputs_read = [t_kd, t_ks, t_qd, t_qi]
                self.b_read = [t_qd, t_kd, t_qi, t_ks, t_b_read]
                return (kd, t_kd), (qd, t_qd), (qi, t_qi), (dec, t_dec), (ks, t_ks)

            def mix(self, got, v_tm, t_v, v0, write):
                (kd, t_kd), (qd, t_qd), (qi, t_qi), (dec, t_dec), (ks, t_ks) = got
                bs, nb, dv = self.block, self.nb, self.dv
                bank = S.next()
                first = [t_kd, t_qd, *bank.free]
                for c in range(NCHUNK):
                    half = slice(64 * (c % 2), 64 * (c % 2) + 64)
                    for j in range(nb):
                        a = (c // 2) * CHUNK + j * bs
                        t_sc = PE.mm(bank.buf[half, a:a + bs], kd.buf[:, c, j, :], qd.buf[:, c * CHUNK + j * bs:c * CHUNK + (j + 1) * bs],
                                     True, True, after=first, signal=(c == NCHUNK - 1 and j == nb - 1))
                        first = []
                kd.free, qd.free = [t_sc], [t_sc]
                sc = self.sc.next()
                for i in range(2):
                    half = slice(64 * i, 64 * i + 64)
                    to = sc.buf[half, :, half]
                    mask, scores = (a[half, 0:4 * CHUNK].rearrange("p (c t) -> p c t", t=CHUNK)
                                    for a in (self.mask, bank.buf))
                    t_m = DVE.do(lambda e, to=to, mask=mask, scores=scores: e.copy_predicated(to, mask, scores),
                                 after=[t_sc, *sc.free])
                bank.free = [t_m]
                bank = S.next()
                for i in range(4):
                    t = PE.tr(bank.buf[:, i * P:(i + 1) * P], ks.buf[:, i * P:(i + 1) * P], ident[:, :],
                              after=[t_ks, ident_token, *bank.free], signal=(i == 3))
                ks.free = [t]
                kst = self.kst.next()
                t_kst = SC.act(kst.buf[:, :, :].rearrange("p a b -> p (a b)"), bank.buf, ACT.Copy, after=[t, *kst.free])
                bank.free = [t_kst]
                st = self.st.next()
                per = 2 * (T // dv)
                t_st = None
                for c0 in range(0, NCHUNK - 1, per):
                    banks = [S.next(), S.next()]
                    group = range(c0, min(c0 + per, NCHUNK - 1))
                    places = [banks[c % 2].buf[:, (c - c0) // 2 * dv:(c - c0) // 2 * dv + dv] for c in group]
                    for c, place in zip(group, places):
                        half = slice(64 * (c % 2), 64 * (c % 2) + 64)
                        t = PE.mm(place, kst.buf[half, c // 2, :], v_tm[half, c // 2, v0:v0 + dv], True, True,
                                  after=[t_kst, t_v, *banks[c % 2].free], signal=(c == group[-1]))
                    for c, place in zip(group, places):
                        if c == 0:
                            t_st = DVE.copy(st.buf[:, 1, :], place, after=[t, *st.free])
                        else:
                            t_st = DVE.stt(st.buf[:, c + 1, :], st.buf[:, c, :], dec.buf[:, c:c + 1], place, ALU.mult,
                                           ALU.add, after=[t, t_st, t_dec])
                    banks[0].free = banks[1].free = [t_st]
                kst.free, dec.free = [t], [t_st]
                for d in range(dv // P):
                    o = O.next()
                    first = [t_m, t_st, t_qi, t_v, *o.free]
                    for i in range(4):
                        PE.mm(o.buf[:, i * P:(i + 1) * P], v_tm[:, i, v0 + d * P:v0 + (d + 1) * P], sc.buf[:, i, :],
                              True, False, after=first)
                        for c in range(max(2 * i, 1), 2 * i + 2):
                            cs = slice(c * CHUNK, (c + 1) * CHUNK)
                            t = PE.mm(o.buf[:, cs], st.buf[:, c, d * P:(d + 1) * P], qi.buf[:, cs], False,
                                      c == 2 * i + 1, signal=(c == NCHUNK - 1))
                    write(d, o, t)
                sc.free, st.free, qi.free = [t], [t], [t]

        while stream.seen < 16:
            stream.step()
        for k in range(KT):
            square_sum(k)
        stream.fold()
        norm_to_h("norm_mix0", 0, 0)

        phase_start = barrier()
        b_all = at("hg_b", 0, [P, 8, T])
        k_all = at("hg_k", 16 * KB, [P, 8, T])
        v_tm = at("hg_v_tm", 32 * KB, [P, 4, D])
        gated = Gated("hg", 48 * KB, P, 16, phase_start)
        assert gated.end <= 101 * KB, gated.end
        q_sb = Ring([at("hg_q_sb", gated.end, [P, T])], phase_start)
        v_done = [None]

        def store_v(group):
            def put(tok, bank, t):
                v_done[0] = SC.act(v_tm[:, tok, group * T:(group + 1) * T], bank.buf, ACT.Copy, after=[t, *phase_start])
                bank.free = [v_done[0]]
            return put

        for g in range(2):
            tm_product("hg_v", g, store_v(g))
        for h in range(8):
            bank, t = fm_product("hg_f", h)
            t1 = SC.act(b_all[:, h, :], bank.buf, ACT.Sigmoid, after=[t, *phase_start])
            t2 = SC.act(k_all[:, h, :], bank.buf, ACT.Sigmoid, scale=-1.0, after=[t, *phase_start])
            bank.free = [t2]
            t_k = DVE.ts(k_all[:, h, :], k_all[:, h, :], one_m_lb[:, h:h + 1], None, ALU.mult, after=[t2, lb_token])
        b_ready = [None] * 8
        for h in range(8):
            t = SC.act(b_all[:, h, :], b_all[:, h, :], ACT.Ln, scale=one_m_lb[:, h:h + 1], bias=lb[:, h:h + 1], after=[t1, lb_token])
            b_ready[h] = (t, t_k)
        o_ready = [None] * 8
        o_free = [None] * 8

        def store_head(h):
            def put(d, o, t_o):
                sq, r = gated.sq.next(), gated.rstd.next()
                t = SC.act(sq.buf[:, :], o.buf, ACT.Square, after=[t_o, *sq.free])
                bank = S.next()
                t = PE.mm(bank.buf, gated.mean[:, :], sq.buf[:, :], True, True, after=[t, gated.const, *bank.free], signal=True)
                sq.free = [t]
                t = inverse_rms(r.buf[:, :], bank, t, after=r.free)
                o_ready[h] = DVE.stt(b_all[:, h, :], o.buf, col("gnorm"), r.buf[:, :], ALU.mult, ALU.mult,
                                     after=[t, cols_token, *o_free[h]])
                o.free = [o_ready[h]]
                r.free = [o_ready[h]]
            return put

        waiting = None
        for h in range(9):
            if h < 8:
                bank, t = fm_product("hg_q", h)
                q = q_sb.next()
                t_q = SC.act(q.buf[:, :], bank.buf, ACT.Copy, after=[t, *q.free])
                bank.free = [t_q]
                lg, t_k = b_ready[h]
                sq = gated.sq.next()
                t = SC.act(sq.buf[:, :], b_all[:, h, :], ACT.Copy, after=[lg, *sq.free])
                t_b = gated.running_sum(b_all[:, h, :], sq.buf[:, :], [t])
                sq.free = [t_b]
                got = gated.factors(q.buf[:, :], t_q, k_all[:, h, :], t_k, b_all[:, h, :], t_b)
                q.free = gated.inputs_read
                o_free[h] = gated.b_read
            if waiting is not None:
                gated.mix(waiting, v_tm, v_done[0], (h - 1) * P, store_head(h - 1))
            waiting = got
        on_start = barrier()
        on_hi = at("hg_on_hi", 32 * KB, [P, 8, T], F32R)
        on_lo = at("hg_on_lo", 48 * KB, [P, 8, T], F32R)
        g_sb = Ring([at(f"hg_g{i}", (64 + 2 * i) * KB, [P, T]) for i in range(3)], on_start)
        on_ready = [None] * 8
        for h in range(8):
            bank, t = fm_product("hg_g", h)
            s = g_sb.next()
            t = SC.act(s.buf[:, :], bank.buf, ACT.Silu, after=[t, *s.free])
            bank.free = [t]
            t = DVE.tt(s.buf[:, :], s.buf[:, :], b_all[:, h, :], ALU.mult, after=[t, o_ready[h]])
            t_hi, t_lo = split_into(on_hi, on_lo, h, s.buf[:, :], [t], on_start if h == 0 else ())
            s.free = [t_hi, t_lo]
            on_ready[h] = t_lo
        for n in range(KT):
            bank, t = fm_product("hg_out", n, src_hi=on_hi, src_lo=on_lo, ready=on_ready)
            residual(n, bank, t, mod[:, 0, 16 + n:17 + n], [stream.mod_token[0]])
        norm_to_h("norm_ffn0", 0, 1)
        ffn("up0", "down0", lambda n: mod[:, 0, 40 + n:41 + n], ("conv_w0", "conv_b0"))
        stream.fold()
        norm_to_h("norm_mix1", 1, 0)

        phase_start = barrier()
        o_hi = at("nsa_o_hi", 0, [P, 8, T], F32R)
        o_lo = at("nsa_o_lo", 16 * KB, [P, 8, T], F32R)
        v_sw = at("nsa_v_sw", 32 * KB, [P, 4, T])
        k_sw = at("nsa_k_sw", 40 * KB, [P, 4, T])
        cw1 = at("cmp_w1", 48 * KB, [P, 2, CMP_LEN, HD])
        kv_c = at("cmp_kv", 64 * KB, [P, 4, T])
        probs = Ring([at(f"probs{i}", (48 + 5 * i) * KB, [P, 1280]) for i in range(4)])
        probs_t = Ring([at(f"probs_t{i}", (68 + 5 * i) * KB, [P, 1280]) for i in range(2)])
        q_sb = Ring([at(f"nsa_q{i}", (78 + 2 * i) * KB, [P, T]) for i in range(2)], phase_start)
        bias_h = Ring([at(f"bias{i}", (82 + 2 * i) * KB, [P, T]) for i in range(2)], phase_start)
        dist = at("dist", 86 * KB, [P, T])
        pc_t = Ring([at("pc_t", 88 * KB, [NCMP, T])], phase_start)
        small = [90 * KB]

        def little(name, shape, dt=F32):
            t = at(f"nsa_{name}", small[0], shape, dt)
            small[0] += (int(np.prod(shape[1:])) * 4 + 31) // 32 * 32
            return t

        dist_c = little("dist_c", [P, 4, NCMP])
        pc = Ring([little(f"pc{i}", [P, 4, NCMP]) for i in range(2)], phase_start)
        gate = little("gate", [P, 4, 48])
        valid0 = little("valid0", [P, 1])
        cw2 = little("cmp_w2", [HD, 2, HD])
        z = little("z", [HD, 2, 2, 2, NCMP])
        pe_bias = little("pe_bias", [HD, 2])
        kc_t = little("kc_t", [P, 2, NCMP])
        vc_n = little("vc_n", [NCMP, NSA_GROUPS, HD])
        maxes = Ring([little(f"maxes{i}", [P, 3, 4]) for i in range(2)], phase_start)
        sums = Ring([little(f"sums{i}", [P, 3, 4]) for i in range(2)], phase_start)
        nmax = Ring([little(f"nmax{i}", [P, 3, 4]) for i in range(2)], phase_start)
        assert small[0] <= 101 * KB, small[0]

        for half in range(2):
            SP.do(lambda e, half=half: e.dma_start(cw1[64 * half:64 * half + 64, :, :, :], dram["cmp_w1"]),
                  phase_start, dma_sem=cmp_landed)
        SP.do(lambda e: e.dma_start(cw2[:, :, :], dram["cmp_w2"]), phase_start, dma_sem=cmp_landed)
        cmp_token = (cmp_landed, 48)

        t = GP.do(lambda e: e.iota(dist[:, :], pattern=[[-1, T]], base=384, channel_multiplier=1,
                                   allow_small_or_imprecise_dtypes=True), phase_start)
        dist_token = GP.do(lambda e: e.affine_select(out=dist[:, :], in_=dist[:, :], compare_op=ALU.is_ge, fill=MASKED,
                                                     base=384, pattern=[[-1, T]], channel_multiplier=1), [t])
        t = GP.do(lambda e: e.iota(dist_c[:, :, :], pattern=[[P, 4], [-CMP_STRIDE, NCMP]], base=0, channel_multiplier=1,
                                   allow_small_or_imprecise_dtypes=True), phase_start)
        t = GP.ts(dist_c[:, :, :], dist_c[:, :, :], -(CMP_LEN - 1) / 2.0, None, ALU.add, after=[t])
        distc_token = GP.do(lambda e: e.affine_select(out=dist_c[:, :, :], in_=dist_c[:, :, :], compare_op=ALU.is_ge,
                                                      fill=MASKED, base=-(CMP_LEN - 1),
                                                      pattern=[[P, 4], [-CMP_STRIDE, NCMP]], channel_multiplier=1), [t])
        t = GP.memset(valid0[:, :], 1.0, after=phase_start)
        valid_token = GP.do(lambda e: e.affine_select(out=valid0[:, :], in_=valid0[:, :], compare_op=ALU.is_ge, fill=0.0,
                                                      base=-(CMP_LEN - 1), pattern=[[0, 1]], channel_multiplier=1), [t])

        v_done = [None]

        def put_v(tok, bank, t):
            v_done[0] = SC.act(v_sw[:, tok, :], bank.buf, ACT.Copy, after=[t, *phase_start])
            bank.free = [v_done[0]]

        tm_product("nsa_v", 0, put_v)
        unit = stream.take("nsa_gate", 0)
        bank = G.next()
        for tok in range(4):
            c = slice(tok * P, (tok + 1) * P)
            for k in range(KT):
                w = slice(48 * k, 48 * k + 48)
                out = bank.buf[:, 48 * tok:48 * tok + 48]
                PE.mm(out, h_hi[:, k, c], unit[2][:, w], k == 0, False, after=[unit[4], *bank.free])
                PE.mm(out, h_hi[:, k, c], unit[3][:, w], False, False)
                t = PE.mm(out, h_lo[:, k, c], unit[2][:, w], False, k == KT - 1, signal=(k == KT - 1))
        stream.done(unit, t)
        t = SC.act(gate[:, :, :].rearrange("p a b -> p (a b)"), bank.buf[:, 0:192], ACT.Sigmoid, after=[t, *phase_start])
        bank.free = [t]
        g0 = gate[:, 0, :].rearrange("p (h b) -> p h b", b=3)[:, :, 0:1]
        gate_token = DVE.ts(g0, g0, valid0[:, 0:1], None, ALU.mult, after=[t, valid_token])

        t_kv = None
        for i in range(8):
            bank, t = fm_product("nsa_kv", i)
            dst = kv_c[:, i, :] if i < 4 else k_sw[:, i - 4, :]
            t_kv = SC.act(dst, bank.buf, ACT.Copy, after=[t, *phase_start])
            bank.free = [t_kv]
            if i == 3:
                t_kvc = t_kv
                zb = [S.next(), S.next()]
                pb = S.next()
                for kv in range(2):
                    for l in range(CMP_LEN):
                        t_pe = PE.mm(pb.buf[0:HD, kv:kv + 1], cw1[0:HD, kv, l, :], col("pe", 32 * kv + l)[0:HD, :],
                                     l == 0, l == CMP_LEN - 1, after=[cmp_token, cols_token, *pb.free],
                                     signal=(l == CMP_LEN - 1))
                t_pe = DVE.copy(pe_bias[:, :], pb.buf[0:HD, 0:2], after=[t_pe, *phase_start])
                pb.free = [t_pe]
                for kv in range(2):
                    for par in range(2):
                        rows = slice(64 * par, 64 * par + 64)
                        a = kv * 2 * NCMP
                        for l in range(CMP_LEN):
                            rhs = kv_c[rows, 2 * kv:2 * kv + 2, l:l + CMP_STRIDE * (NCMP - 1) + 1:CMP_STRIDE]
                            t = PE.mm(zb[par].buf[0:HD, a:a + 2 * NCMP].rearrange("p (a b) -> p a b", a=2), cw1[rows, kv, l, :], rhs,
                                      l == 0, l == CMP_LEN - 1, after=[t_kvc, *zb[par].free], signal=(l == CMP_LEN - 1))
                for kv in range(2):
                    a = kv * 2 * NCMP
                    for par in range(2):
                        t = SC.act(z[:, kv, par, :, :].rearrange("p b n -> p (b n)"), zb[par].buf[0:HD, a:a + 2 * NCMP],
                                   ACT.Silu, bias=pe_bias[:, kv:kv + 1], after=[t, t_pe, *phase_start])
                zb[0].free = zb[1].free = [t]
                t_z = t
                kb = S.next()
                for par in range(2):
                    t = PE.mm(kb.buf[64 * par:64 * par + 64, 0:2 * NCMP], cw2[:, 0, :],
                              z[:, 0, par, :, :].rearrange("p b n -> p (b n)"), True, True,
                              after=[t_z, *kb.free], signal=True)
                t_kc = DVE.copy(kc_t[:, :, :].rearrange("p b n -> p (b n)"), kb.buf[:, 0:2 * NCMP], after=[t, *phase_start])
                kb.free = [t_kc]
                vb = S.next()
                for g in range(NSA_GROUPS):
                    t = PE.mm(vb.buf[0:NCMP, HD * g:HD * g + HD], z[:, 1, g % 2, g // 2, :], cw2[:, 1, :], True, True,
                              after=[t_z, *vb.free], signal=True)
                t_vc = DVE.copy(vc_n[:, :, :].rearrange("p g d -> p (g d)"), vb.buf[0:NCMP, 0:4 * HD], after=[t, *phase_start])
                vb.free = [t_vc]
                compressed = barrier()
                for r in (probs, probs_t):
                    for s in r.slots:
                        s.free = list(compressed)

        OFF_Q = [0, 128, 384, 768]
        OFF_K = [0, 512, 1024, 896]
        scale = HD ** -0.5

        def softmax_stage(head, half, q, t_q):
            g = head // 4
            rows = slice(64 * half, 64 * half + 64)
            slope = 2.0 ** (-8.0 * (head + 1) / NSA_HEADS)
            bias = bias_h.next()
            t_bias = GP.ts(bias.buf[:, :], dist[:, :], -slope / scale, None, ALU.mult, after=[dist_token, *bias.free])
            mx, sm, nm = maxes.next(), sums.next(), nmax.next()
            bank = S.next()
            for i in range(4):
                t = PE.mm(bank.buf[:, NCMP * i:NCMP * (i + 1)], q.buf[rows, i * P:(i + 1) * P], kc_t[rows, g // 2, :],
                          True, True, after=[t_q, t_kc, *bank.free], signal=(i == 3))
            c = pc.next()
            cb = c.buf[:, :, :]
            t = DVE.stt(cb.rearrange("p a n -> p (a n)"), dist_c[:, :, :].rearrange("p a n -> p (a n)"), -slope / scale,
                        bank.buf[:, 0:4 * NCMP], ALU.mult, ALU.add, after=[t, distc_token, *c.free])
            bank.free = [t]
            t_mc = DVE.do(lambda e: e.tensor_reduce(mx.buf[:, 0, :], cb, AX.X, ALU.max), after=[t, *mx.free])
            t = DVE.tt(cb, cb, mx.buf[:, 0, :].unsqueeze(2).to_broadcast([P, 4, NCMP]), ALU.subtract, after=[t_mc])
            t = SC.act(cb, cb, ACT.Exp, scale=scale, after=[t])
            t_sc = DVE.do(lambda e: e.tensor_reduce(sm.buf[:, 0, :], cb, AX.X, ALU.add), after=[t, *sm.free])
            pr = []
            t_sum = []
            for br in range(2):
                p = probs.next()
                t_max = None
                for i in range(4):
                    n = (i + 1) * P
                    bank = S.next()
                    t = PE.mm(bank.buf[:, 0:n], q.buf[rows, i * P:(i + 1) * P], k_sw[rows, 2 * br + g // 2, 0:n],
                              True, True, after=[t_q, t_kv, *bank.free], signal=True)
                    dst = p.buf[:, OFF_Q[i]:OFF_Q[i] + n]
                    b = bias.buf[:, 384 - P * i:T]
                    m = mx.buf[:, 1 + br, i:i + 1]
                    t_max = DVE.do(lambda e, dst=dst, bank=bank, n=n, b=b, m=m: e.tensor_tensor_reduce(
                        dst, bank.buf[:, 0:n], b, 1.0, -3.0e38, ALU.add, ALU.max, m),
                        after=[t, t_bias, *p.free, *mx.free])
                    bank.free = [t_max]
                t_neg = DVE.ts(nm.buf[:, 1 + br, :], mx.buf[:, 1 + br, :], -scale, None, ALU.mult, after=[t_max, *nm.free])
                for i in range(4):
                    n = (i + 1) * P
                    dst = p.buf[:, OFF_Q[i]:OFF_Q[i] + n]
                    t = SC.act(dst, dst, ACT.Exp, scale=scale, bias=nm.buf[:, 1 + br, i:i + 1],
                               accum_out=sm.buf[:, 1 + br, i:i + 1], after=[t_neg, *sm.free])
                pr.append(p)
                t_sum.append(t)
            bias.free = [t_max]
            sv = sm.buf[:, :, :].rearrange("p a b -> p (a b)")
            t = DVE.do(lambda e: e.reciprocal(sv, sv), after=[t_sc, *t_sum])
            gv = gate[:, :, 3 * head:3 * head + 3].rearrange("p i b -> p b i")
            t_f = DVE.tt(sm.buf[:, :, :], sm.buf[:, :, :], gv, ALU.mult, after=[t, gate_token])
            t_pc = DVE.tt(cb, cb, sm.buf[:, 0, :].unsqueeze(2).to_broadcast([P, 4, NCMP]), ALU.mult, after=[t_f])
            t_p = []
            for br in range(2):
                for i in range(4):
                    n = (i + 1) * P
                    dst = pr[br].buf[:, OFF_Q[i]:OFF_Q[i] + n]
                    lane = DVE
                    t = lane.ts(dst, dst, sm.buf[:, 1 + br, i:i + 1], None, ALU.mult, after=[t_f])
                t_p.append(t)
            mx.free, nm.free, sm.free = [t_p[1]], [t_p[1]], [t_p[1]]
            return head, half, (c, t_pc), list(zip(pr, t_p)), q

        def value_stage(got, o):
            head, half, (c, t_pc), pr, q = got
            g = head // 4
            rows = slice(64 * half, 64 * half + 64)
            bank = S.next()
            for i in range(4):
                t = PE.tr(bank.buf[0:NCMP, i * P:(i + 1) * P], c.buf[:, i, :], ident[:, :],
                          after=[t_pc, ident_token, *bank.free], signal=(i == 3))
            c.free = [t]
            pt = pc_t.next()
            t = DVE.copy(pt.buf[:, :], bank.buf[0:NCMP, :], after=[t, *pt.free])
            bank.free = [t]
            t = PE.mm(o.buf[rows, :], vc_n[:, g, :], pt.buf[:, :], True, False, after=[t, t_vc, *o.free], signal=True)
            pt.free = [t]
            for br in range(2):
                p, t_p = pr[br]
                banks = [G.next() for _ in range(3)]
                place = {0: (0, 0), 1: (1, 0), 3: (1, 384), 2: (2, 0)}
                tok = [None] * 3
                for j in (0, 1, 3, 2):
                    b, a = place[j]
                    for i in range(j, 4):
                        src = p.buf[:, OFF_Q[i] + j * P:OFF_Q[i] + (j + 1) * P]
                        dst = banks[b].buf[:, a + (i - j) * P:a + (i - j + 1) * P]
                        tok[b] = PE.tr(dst, src, ident[:, :], after=[t_p, *banks[b].free], signal=(i == 3))
                p.free = [tok[2]]
                pt = probs_t.next()
                ready = []
                for b, (a, n) in enumerate(((0, 512), (512, 512), (1024, 256))):
                    f = (lambda *r, **k: SC.act(r[0], r[1], ACT.Copy, **k)) if b == 0 else DVE.copy
                    ready.append(f(pt.buf[:, a:a + n], banks[b].buf[:, 0:n], after=[tok[b], *pt.free]))
                    banks[b].free = [ready[b]]
                for j in (0, 1, 3, 2):
                    n = T - j * P
                    t = PE.mm(o.buf[rows, j * P:T], v_sw[:, j, 256 * br + HD * g:256 * br + HD * (g + 1)],
                              pt.buf[:, OFF_K[j]:OFF_K[j] + n], False, br == 1 and j == 2,
                              after=[ready[place[j][0]], v_done[0]], signal=(j == 2))
                pt.free = [t]
            return t

        nsa_o_ready = [None] * 8
        heads = [(pair, half, 4 * (2 * (pair // 4) + half) + pair % 4) for pair in range(8) for half in range(2)]
        waiting = []
        o_slot = None
        q_of = {}

        def finish_head(entry):
            global_pair, got = entry
            if got[1] == 0:
                finish_head.o = O.next()
            t = value_stage(got, finish_head.o)
            if got[1] == 1:
                o = finish_head.o
                t_hi = SC.act(o_hi[:, global_pair, :], o.buf, ACT.Copy, after=[t, *phase_start])
                t_lo = DVE.tt(o_lo[:, global_pair, :], o.buf, o_hi[:, global_pair, :].bitcast(F32), ALU.subtract, after=[t_hi])
                o.free = [t_lo]
                nsa_o_ready[global_pair] = t_lo

        for pair, half, head in heads:
            if half == 0:
                bank, t = fm_product("nsa_q", pair)
                q = q_sb.next()
                t_q = SC.act(q.buf[:, :], bank.buf, ACT.Copy, after=[t, *q.free])
                bank.free = [t_q]
            waiting.append((pair, softmax_stage(head, half, q, t_q)))
            if half == 1:
                q.free = [PE.last]
            if len(waiting) > 1:
                finish_head(waiting.pop(0))
        finish_head(waiting.pop(0))
        for n in range(KT):
            bank, t = fm_product("nsa_out", n, src_hi=o_hi, src_lo=o_lo, ready=nsa_o_ready)
            residual(n, bank, t, mod[:, 1, 16 + n:17 + n], [stream.mod_token[1]])
        norm_to_h("norm_ffn1", 1, 1)
        ffn("up1", "down1", lambda n: mod[:, 1, 40 + n:41 + n], ("conv_w1", "conv_b1"))
        normalize_x("final_norm")

        h_dead[0] = PE.last
        for k in range(KT):
            square_sum(k)
        norm_to_h("b_norm_ffn1")
        ffn("bup1", "bdown1", lambda n: 0.5)
        norm_to_h("b_norm_mix")

        phase_start = barrier()
        merged = at("merged", 0, [P, 8, T])
        c_hi = at("c_hi", 32 * KB, [P, 8, T], F32R)
        c_lo = at("c_lo", 48 * KB, [P, 8, T], F32R)
        temps = Ring([at(f"conv_a{i}", (64 + 2 * i) * KB, [P, T])[:, :] for i in range(3)], phase_start)
        temps2 = Ring([at(f"conv_b{i}", (70 + 2 * i) * KB, [P, T])[:, :] for i in range(3)], phase_start)
        c_ready = [None] * 8
        for i in range(8):
            cc, t_cc = fm_product("b_conv", 8 + i)
            cu, t_cu = fm_product("b_conv", 16 + i)
            cb, t_cb = fm_product("b_conv", i)
            a, y = temps.next(), temps2.next()
            t = SC.act(a.buf, cc.buf, ACT.Copy, after=[t_cc, *a.free])
            cc.free = [t]
            t = DVE.tt(a.buf, a.buf, cu.buf, ALU.mult, after=[t, t_cu])
            cu.free = [t]
            t = causal_conv(y.buf, a.buf, [col("b_conv_w", 8 * j + i) for j in range(3)], [t, cols_token], free=y.free)
            a.free = [t]
            t = DVE.tt(y.buf, y.buf, cb.buf, ALU.mult, after=[t, t_cb])
            cb.free = [t]
            t_hi, t_lo = split_into(c_hi, c_lo, i, y.buf, [t], phase_start if i == 0 else ())
            y.free = [t_hi, t_lo]
            c_ready[i] = t_lo
        m_ready = [None] * 8
        for i in range(8):
            ga, t_a = fm_product("b_ga", i)
            yc, t_y = fm_product("b_out_conv", i, src_hi=c_hi, src_lo=c_lo, ready=c_ready)
            a = temps.next()
            t = SC.act(a.buf, ga.buf, ACT.Sigmoid, after=[t_a, *a.free])
            ga.free = [t]
            m_ready[i] = DVE.tt(merged[:, i, :], a.buf, yc.buf, ALU.mult, after=[t, t_y, *phase_start])
            yc.free = [m_ready[i]]
            a.free = [m_ready[i]]

        phase_start = barrier()
        o_all = at("gla_o", 16 * KB, [P, 8, T])
        v_tm = at("gla_v_tm", 32 * KB, [P, 4, D])
        b_all = at("gla_b", 48 * KB, [P, 4, T])
        gup = at("gate_up", 56 * KB, [16, T])
        glr = at("g_lr", 58 * KB, [16, T])
        q_sb = Ring([at("gla_q", 58 * KB, [P, T])])
        k_sb = Ring([at("gla_k", 60 * KB, [P, T])], phase_start)
        gated = Gated("gla", 62 * KB, 256, 64, phase_start)
        assert gated.end <= 101 * KB, gated.end
        SP.do(lambda e: e.dma_start(gup[:, :], dram["gate_w_up"]), phase_start, dma_sem=gup_landed)
        bank, t = fm_product("b_glr", 0)
        t_glr = SC.act(glr[:, :], bank.buf[0:16, :], ACT.Copy, after=[t, *phase_start])
        bank.free = [t_glr]
        b_ready = [None] * 4
        for h in range(4):
            bank = S.next()
            t = PE.mm(bank.buf, gup[:, h * P:(h + 1) * P], glr[:, :], True, True,
                      after=[t_glr, (gup_landed, 16), *bank.free], signal=True)
            zb = b_all[:, h, :]
            s = gated.sq.next()
            t = DVE.ts(zb, bank.buf, col("gate_b", h), None, ALU.add, after=[t, cols_token, *phase_start])
            bank.free = [t]
            t1 = SC.act(s.buf[:, :], zb, ACT.Abs, after=[t, *s.free])
            t1 = SC.act(s.buf[:, :], s.buf[:, :], ACT.Exp, scale=-1.0, after=[t1])
            t1 = SC.act(s.buf[:, :], s.buf[:, :], ACT.Ln, bias=ones[:, 0:1], after=[t1])
            t = DVE.stt(s.buf[:, :], zb, 0.0, s.buf[:, :], ALU.min, ALU.subtract, after=[t1])
            t = DVE.ts(s.buf[:, :], s.buf[:, :], 1.0 / 16.0, None, ALU.mult, after=[t])
            b_ready[h] = gated.running_sum(zb, s.buf[:, :], [t])
            s.free = [b_ready[h]]
            q_sb.slots[0].free = [DVE.last]
        v_done = [None]
        for g in range(2):
            def put(tok, bank, t, g=g):
                v_done[0] = SC.act(v_tm[:, tok, g * T:(g + 1) * T], bank.buf, ACT.Copy, after=[t, *phase_start])
                bank.free = [v_done[0]]
            tm_product("b_v", g, put)

        def store_gla(h):
            outs = []

            def put(d, o, t_o):
                t = SC.act(o_all[:, 2 * h + d, :], o.buf, ACT.Copy, after=[t_o, *phase_start])
                o.free = [t]
                sq = gated.sq.next()
                t_s = SC.act(sq.buf[:, :], o_all[:, 2 * h + d, :], ACT.Square, after=[t, *sq.free])
                outs.append((sq, t_s))
                if d == 0:
                    return
                bank, r = S.next(), gated.rstd.next()
                PE.mm(bank.buf, gated.mean[:, :], outs[0][0].buf[:, :], True, False,
                      after=[outs[0][1], gated.const, *bank.free])
                t = PE.mm(bank.buf, gated.mean[:, :], outs[1][0].buf[:, :], False, True, after=[outs[1][1]], signal=True)
                outs[0][0].free = outs[1][0].free = [t]
                t = inverse_rms(r.buf[:, :], bank, t, after=r.free)
                for i in range(2):
                    n = 2 * h + i
                    o_ready[n] = DVE.stt(o_all[:, n, :], o_all[:, n, :], col("gla_norm", n), r.buf[:, :], ALU.mult,
                                         ALU.mult, after=[t, cols_token])
                r.free = [o_ready[n]]
            return put

        o_ready = [None] * 8
        waiting = None
        for h in range(5):
            if h < 4:
                bank, t = fm_product("b_q", h)
                q, k = q_sb.next(), k_sb.next()
                t_q = SC.act(q.buf[:, :], bank.buf, ACT.Copy, scale=float(P) ** -0.5, after=[t, *q.free])
                bank.free = [t_q]
                bank, t = fm_product("b_k", h)
                t_k = SC.act(k.buf[:, :], bank.buf, ACT.Copy, after=[t, *k.free])
                bank.free = [t_k]
                got = gated.factors(q.buf[:, :], t_q, k.buf[:, :], t_k, b_all[:, h, :], b_ready[h])
                q.free = k.free = gated.inputs_read
            if waiting is not None:
                gated.mix(waiting, v_tm, v_done[0], (h - 1) * 256, store_gla(h - 1))
            waiting = got

        phase_start = barrier()
        g_hi = at("gla_g_hi", 32 * KB, [P, 8, T], F32R)
        g_lo = at("gla_g_lo", 48 * KB, [P, 8, T], F32R)
        m_hi = at("merged_hi", 64 * KB, [P, 8, T], F32R)
        m_lo = at("merged_lo", 80 * KB, [P, 8, T], F32R)
        temps = Ring([at(f"r_sb{i}", (96 + 2 * i) * KB, [P, T])[:, :] for i in range(2)], phase_start)
        g_ready = [None] * 8
        for i in range(8):
            bank, t = fm_product("b_r", i)
            s = temps.next()
            t = SC.act(s.buf, bank.buf, ACT.Silu, after=[t, *s.free])
            bank.free = [t]
            t = DVE.tt(s.buf, s.buf, o_all[:, i, :], ALU.mult, after=[t, o_ready[i]])
            t_hi, t_lo = split_into(g_hi, g_lo, i, s.buf, [t], phase_start if i == 0 else ())
            s.free = [t_hi, t_lo]
            g_ready[i] = t_lo
        mm_ready = [None] * 8
        for i in range(8):
            gb, t_b = fm_product("b_gb", i)
            yg, t_y = fm_product("b_out_gla", i, src_hi=g_hi, src_lo=g_lo, ready=g_ready)
            s = temps.next()
            t = SC.act(s.buf, gb.buf, ACT.Sigmoid, after=[t_b, *s.free])
            gb.free = [t]
            t = DVE.tt(s.buf, s.buf, yg.buf, ALU.mult, after=[t, t_y])
            yg.free = [t]
            t = DVE.tt(s.buf, s.buf, merged[:, i, :], ALU.add, after=[t, m_ready[i]])
            t_hi, t_lo = split_into(m_hi, m_lo, i, s.buf, [t], ())
            s.free = [t_hi, t_lo]
            mm_ready[i] = t_lo
        for n in range(KT):
            bank, t = fm_product("b_o", n, src_hi=m_hi, src_lo=m_lo, ready=mm_ready)
            residual(n, bank, t, 1.0)
        norm_to_h("b_norm_ffn2")
        ffn("bup2", "bdown2", lambda n: 0.5)

        t_r = finish_rms()
        for k in range(KT):
            t = DVE.stt(x[:, k, :], x[:, k, :], col("b_final_norm", k), rstd, ALU.mult, ALU.mult,
                        after=[t_r, x_ready[k], cols_token])
            SP.do(lambda e, k=k: e.dma_start(dram["out"][:, k, :], x[:, k, :]), [t], dma_sem=out_stored)
        SP.do(lambda e: e.wait_ge(out_stored, 16 * KT), signal=False)
        assert max(ends) <= nc.sbuf_usable_end, (max(ends), nc.sbuf_usable_end, arena)
        assert stream.taken == n_w

        block = ctx.enter_context(nc.Block())

        @block.sync
        def _(eng):
            SP.emit(eng)

        @block.tensor
        def _(eng):
            PE.emit(eng)

        @block.vector
        def _(eng):
            DVE.emit(eng)

        @block.scalar
        def _(eng):
            SC.emit(eng)

        @block.gpsimd
        def _(eng):
            GP.emit(eng)


def _tiles(w, cols=None):
    w = w if cols is None else w[:, cols]
    K, N = w.shape
    return np.ascontiguousarray(w.reshape(K // P, P, N // P, P).transpose(2, 1, 0, 3)).reshape(N // P, P, K)


def _wide(w):
    K, N = w.shape
    return np.ascontiguousarray(w.reshape(4, 2, P, N // T, T).transpose(3, 0, 2, 1, 4)).reshape(N // T, 4, P, 2 * T)


def _vec(v):
    return np.asarray(v).reshape(-1, P).T


def kernel(**inputs):
    import concourse.bacc as _bacc
    from concourse.bass_utils import run_bass_kernel_spmd as _run

    a = {k: np.asarray(v) for k, v in inputs.items()}
    hg, nsa, b_in = a["hg_w_in"][0], a["nsa_w_in"][0], a["w_in_2"][0]
    order = [4 * (2 * (p // 4) + half) + p % 4 for p in range(8) for half in range(2)]
    q_cols = np.concatenate([np.arange(HD * h, HD * h + HD) for h in order])
    v_cols = np.concatenate([np.arange(1792, 2048), np.arange(2304, 2560)])
    kv_cols = np.concatenate([np.arange(1024, 1792), np.arange(2048, 2304)])
    glr = np.zeros((D, P), b_in.dtype)
    glr[:, 0:16] = b_in[:, 5120:5136]
    pe = a["nsa_cmp_pe"][0].reshape(2 * CMP_LEN, HD).T
    parts = {
        "c": _vec(a["c"][0]), "norm_mix0": _vec(a["norm_mix"][0]), "norm_ffn0": _vec(a["norm_ffn"][0]),
        "norm_mix1": _vec(a["norm_mix"][1]), "norm_ffn1": _vec(a["norm_ffn"][1]), "final_norm": _vec(a["final_norm"]),
        "b_norm_ffn1": _vec(a["norm_ffn1_g_2"][0]), "b_norm_mix": _vec(a["norm_mix_g_2"][0]),
        "b_norm_ffn2": _vec(a["norm_ffn2_g_2"][0]), "b_final_norm": _vec(a["final_norm_g_2"]),
        "ada_b": _vec(a["ada_b"].reshape(-1)), "gnorm": _vec(a["hg_gnorm"][0]), "hg_lb": _vec(a["hg_lb"].reshape(-1)),
        "conv_w0": _vec(a["ffn_conv_w"][0].reshape(-1)), "conv_b0": _vec(a["ffn_conv_b"][0]),
        "conv_w1": _vec(a["ffn_conv_w"][1].reshape(-1)), "conv_b1": _vec(a["ffn_conv_b"][1]),
        "b_conv_w": _vec(a["conv_w_2"][0].reshape(-1)), "gate_b": _vec(a["gate_b_2"][0]),
        "gla_norm": _vec(a["gla_norm_g_2"][0]), "pe": np.concatenate([pe, pe], axis=0),
    }
    ada = a["ada_w"].reshape(2, 4, 2, P, 12, T).transpose(0, 4, 1, 3, 2, 5)
    arrays = {
        "cols": np.concatenate([parts[n] for n in COLS], axis=1),
        "x": np.ascontiguousarray(a["x"][0].T.reshape(KT, P, T).transpose(1, 0, 2)),
        "ada": np.ascontiguousarray(ada).reshape(2, 12, 4, P, 2 * T),
        "hg_q": _tiles(hg[:, 0:D]), "hg_f": _tiles(hg[:, D:2 * D]), "hg_v": _wide(hg[:, 2 * D:3 * D]),
        "hg_g": _tiles(hg[:, 3 * D:4 * D]), "hg_out": _tiles(a["hg_w_out"][0]),
        "nsa_q": _tiles(nsa, q_cols), "nsa_kv": _tiles(nsa, kv_cols), "nsa_v": _wide(nsa[:, v_cols]),
        "nsa_gate": np.ascontiguousarray(nsa[:, 2560:2608].reshape(8, P, 48).transpose(1, 0, 2)).reshape(1, P, 8 * 48),
        "nsa_out": _tiles(a["nsa_w_out"][0][q_cols, :]),
        "cmp_w1": np.ascontiguousarray(a["nsa_cmp_w1"][0].reshape(2, CMP_LEN, HD, HD).transpose(2, 0, 1, 3)),
        "cmp_w2": np.ascontiguousarray(a["nsa_cmp_w2"][0].transpose(1, 0, 2)),
        "up0": _tiles(a["ffn_w_up"][0]), "down0": _tiles(a["ffn_w_down"][0]),
        "up1": _tiles(a["ffn_w_up"][1]), "down1": _tiles(a["ffn_w_down"][1]),
        "bup1": _tiles(a["ffn1_w_gu_2"][0]), "bdown1": _tiles(a["ffn1_w_down_2"][0]),
        "bup2": _tiles(a["ffn2_w_gu_2"][0]), "bdown2": _tiles(a["ffn2_w_down_2"][0]),
        "b_conv": _tiles(b_in[:, 0:3 * D]), "b_q": _tiles(b_in[:, 3072:3584]), "b_k": _tiles(b_in[:, 3584:4096]),
        "b_v": _wide(b_in[:, 4096:5120]), "b_glr": _tiles(glr), "b_r": _tiles(b_in[:, 5136:6160]),
        "b_ga": _tiles(b_in[:, 6160:7184]), "b_gb": _tiles(b_in[:, 7184:8208]),
        "b_out_conv": _tiles(a["w_out_conv_2"][0]), "b_out_gla": _tiles(a["w_out_gla_2"][0]),
        "b_o": _tiles(a["w_o_2"][0]), "gate_w_up": a["gate_w_up_2"][0],
    }
    nc = _bacc.Bacc("TRN2", target_bir_lowering=False, num_devices=1)
    dram = {n: nc.dram_tensor(f"in_{n}", v.shape, mybir.dt.from_np(v.dtype), kind="ExternalInput").ap()
            for n, v in arrays.items()}
    dram["out"] = nc.dram_tensor("out_t", (P, KT, T), F32, kind="ExternalOutput").ap()
    build(nc, dram)
    r = _run(nc, [{f"in_{n}": np.ascontiguousarray(v) for n, v in arrays.items()}], core_ids=[0])
    out = r.results[0]["out_t"]
    return np.ascontiguousarray(out.transpose(2, 1, 0)).reshape(1, T, D)
```

```python
import numpy as np
import concourse.bass as bass
from concourse import mybir
from contextlib import ExitStack

ALU = mybir.AluOpType
ACT = mybir.ActivationFunctionType
F32 = mybir.dt.float32
F32R = mybir.dt.float32r
U32 = mybir.dt.uint32
AX = mybir.AxisListType

P = 128
T = 512
D = 1024
KT = D // P
FF = 2816
FT = FF // P
UNIT = 1024
RAW_SLOTS = 5
SPLIT_SLOTS = 4
AHEAD = 3
EPS = 1e-6
CHUNK = 64
NCHUNK = T // CHUNK
NSA_HEADS, NSA_GROUPS, HD = 16, 4, 64
CMP_LEN, CMP_STRIDE = 32, 16
NCMP = (T - CMP_LEN) // CMP_STRIDE + 1
MASKED = 1e30

COLS = {}


def _columns():
    at = 0
    for name, n in (("c", 8), ("norm_mix0", 8), ("norm_ffn0", 8), ("norm_mix1", 8), ("norm_ffn1", 8),
                    ("final_norm", 8), ("b_norm_ffn1", 8), ("b_norm_mix", 8), ("b_norm_ffn2", 8),
                    ("b_final_norm", 8), ("ada_b", 96), ("gnorm", 1), ("hg_lb", 16),
                    ("conv_w0", 66), ("conv_b0", 22), ("conv_w1", 66), ("conv_b1", 22),
                    ("b_conv_w", 24), ("gate_b", 4), ("gla_norm", 8), ("pe", 64)):
        COLS[name] = (at, n)
        at += n
    return at


NCOLS = _columns()


class Lane:

    def __init__(self, name, sem):
        self.name, self.sem, self.count, self.steps, self.met = name, sem, 0, [], {}

    def do(self, fn, after=(), signal=True, dma_sem=None):
        waits = {}
        for token in after:
            if token is None:
                continue
            sem, value = token
            if value > self.met.get(sem.name, 0):
                self.met[sem.name] = value
                waits[sem.name] = (sem, value)
        if dma_sem is not None:
            self.steps.append((list(waits.values()), fn, dma_sem, 16))
            return None
        self.steps.append((list(waits.values()), fn, self.sem if signal else None, 1))
        if signal:
            self.count += 1
        return (self.sem, self.count)

    @property
    def last(self):
        return (self.sem, self.count) if self.count else None

    def emit(self, eng):
        for waits, fn, sem, n in self.steps:
            for s, v in waits:
                eng.wait_ge(s, v)
            ins = fn(eng)
            if sem is not None:
                ins.then_inc(sem, n)

    def tt(self, out, a, b, op, after=()):
        return self.do(lambda e: e.tensor_tensor(out, a, b, op), after)

    def ts(self, out, a, s1, s2, op0, op1=None, after=()):
        if op1 is None:
            return self.do(lambda e: e.tensor_scalar(out, a, s1, None, op0), after)
        return self.do(lambda e: e.tensor_scalar(out, a, s1, s2, op0, op1), after)

    def stt(self, out, a, s, b, op0, op1, after=()):
        return self.do(lambda e: e.scalar_tensor_tensor(out=out, in0=a, scalar=s, in1=b, op0=op0, op1=op1), after)

    def copy(self, out, a, after=()):
        return self.do(lambda e: e.tensor_copy(out, a), after)

    def memset(self, out, v, after=()):
        return self.do(lambda e: e.memset(out, v), after)

    def act(self, out, a, f, after=(), **kw):
        return self.do(lambda e: e.activation(out, a, f, **kw), after)

    def mm(self, out, lhsT, rhs, start, stop, after=(), signal=False):
        return self.do(lambda e: e.matmul(out, lhsT, rhs, start=start, stop=stop), after, signal)

    def tr(self, out, a, ident, after=(), signal=False):
        return self.do(lambda e: e.transpose(out, a, ident), after, signal)


class Slot:

    def __init__(self, buf, free=()):
        self.buf, self.free = buf, list(free)


class Ring:
    def __init__(self, bufs, free=()):
        self.slots, self.at = [Slot(b, free) for b in bufs], 0

    def next(self):
        s = self.slots[self.at % len(self.slots)]
        self.at += 1
        return s


def stream_plan():
    ada = [[("a", "ada", (l, g, kp), UNIT) for g in range(12) for kp in range(4)] for l in range(2)]

    def fm(name, tiles):
        return [("w", name, (n,), UNIT) for n in tiles]

    def mix(main, extra):
        out, e = [], 0
        for i, u in enumerate(main):
            out.append(u)
            want = (i + 1) * len(extra) // len(main)
            out += extra[e:want]
            e = want
        return out

    def tm(name, groups):
        return [("w", name, (g, kp), UNIT) for g in groups for kp in range(4)]

    def down(name):
        return [("w", name, (n, k0), min(8, FT - k0) * P) for n in range(KT) for k0 in range(0, FT, 8)]

    def up(name):
        return fm(name, [t for j in range(FT) for t in (j, FT + j)])

    heads = [u for h in range(8) for name in ("hg_f", "hg_q", "hg_g") for u in fm(name, [h])]
    values = tm("hg_v", range(2))
    plan = ada[0][:15] + values[:1] + ada[0][15:16] + values[1:4]
    plan += mix(values[4:] + heads, ada[0][16:]) + fm("hg_out", range(8))
    plan += mix(up("up0") + down("down0"), ada[1])
    plan += tm("nsa_v", range(1)) + [("w", "nsa_gate", (0,), 8 * 48)]
    plan += fm("nsa_kv", (0, 1, 2, 3, 4, 6)) + fm("nsa_q", range(4)) + fm("nsa_kv", (5, 7)) + fm("nsa_q", range(4, 8))
    plan += fm("nsa_out", range(8))
    plan += up("up1") + down("down1")
    plan += up("bup1") + down("bdown1")
    plan += fm("b_conv", [8 * s + i for i in range(8) for s in (1, 2, 0)])
    for i in range(8):
        plan += fm("b_ga", [i]) + fm("b_out_conv", [i])
    plan += fm("b_glr", [0])
    for h in range(4):
        plan += tm("b_v", [h // 2]) if h % 2 == 0 else []
        plan += fm("b_k", [h]) + fm("b_q", [h]) + fm("b_r", [2 * h, 2 * h + 1])
    for i in range(8):
        plan += fm("b_gb", [i]) + fm("b_out_gla", [i])
    plan += fm("b_o", range(8)) + up("bup2") + down("bdown2")
    return plan


def build(nc, dram):
    plan = stream_plan()
    with ExitStack() as ctx:
        def sem(name):
            return ctx.enter_context(nc.semaphore(name))

        PE, DVE, SC, GP, SP = (Lane(n, sem(f"{n}_done")) for n in ("pe", "dve", "act", "pool", "sp"))
        raw_landed = [sem(f"raw_landed{i}") for i in range(RAW_SLOTS)]
        x_landed, cols_landed, cmp_landed, gup_landed = (sem(n) for n in ("x_landed", "cols_landed", "cmp_landed", "gup_landed"))
        out_stored = sem("out_stored")

        top = [(nc.sbuf_base + 31) // 32 * 32]

        def perm(name, shape, dt):
            size = int(np.prod(shape[1:])) * 4
            t = nc.alloc_sbuf_tensor_at(name, shape, dt, offset=top[0])
            top[0] += (size + 31) // 32 * 32
            return t

        x = perm("x", [P, KT, T], F32)
        h_at = top[0]
        h_hi = perm("h_hi", [P, KT, T], F32R)
        h_lo = perm("h_lo", [P, KT, T], F32R)
        hh32 = nc.alloc_sbuf_tensor_at("h_hi_f32", [P, KT, T], F32, offset=h_at)
        hl32 = nc.alloc_sbuf_tensor_at("h_lo_f32", [P, KT, T], F32, offset=h_at + KT * T * 4)
        raw = [perm(f"raw{i}", [P, UNIT], F32) for i in range(RAW_SLOTS)]
        w_hi = [perm(f"w_hi{i}", [P, UNIT], F32R) for i in range(SPLIT_SLOTS)]
        w_lo = [perm(f"w_lo{i}", [P, UNIT], F32R) for i in range(SPLIT_SLOTS)]
        ada_acc = [perm(f"ada_acc{i}", [P, T], F32) for i in range(2)]
        cols = perm("cols", [P, NCOLS + 2], F32)
        mod = perm("mod", [P, 2, 48], F32)
        gain = perm("gain", [P, KT], F32)
        ones = perm("ones", [P, P], F32)
        mean_d = perm("mean_d", [P, P], F32)
        ident = perm("ident", [P, P], F32)
        c_act = perm("c_act", [P, KT], F32)
        eps = cols[:, NCOLS:NCOLS + 1]
        table_probe = cols[:, NCOLS + 1:NCOLS + 2]
        lb = perm("lb", [P, 8], F32)
        one_m_lb = perm("one_m_lb", [P, 8], F32)
        arena = top[0]
        ends = [arena]

        def at(name, offset, shape, dt=F32):
            size = int(np.prod(shape[1:])) * 4
            ends.append(arena + offset + size)
            return nc.alloc_sbuf_tensor_at(name, shape, dt, offset=arena + offset)

        KB = 1024
        psum = [ctx.enter_context(nc.psum_tensor(f"bank{i}", [P, T], F32)) for i in range(8)]
        G = Ring([psum[i][:, :] for i in range(4)])
        S = Ring([psum[i][:, :] for i in range(4, 7)])
        O = Ring([psum[7][:, :]])

        def col(name, i=0, n=1):
            a, _ = COLS[name]
            return cols[:, a + i:a + i + n]

        class Stream:
            def __init__(self):
                self.read = 0
                self.seen = 0
                self.taken = 0
                self.finished = 0
                self.raw_free = [[] for _ in range(RAW_SLOTS)]
                self.split_free = [[] for _ in range(SPLIT_SLOTS)]
                self.n_split = 0
                self.ready = []
                self.sums = []
                self.acc_free = [[], []]
                self.n_groups = 0
                self.mod_token = {}

            def load(self):
                while self.read < len(plan) and self.read < self.seen + RAW_SLOTS:
                    kind, name, index, n = plan[self.read]
                    s = self.read % RAW_SLOTS
                    src = dram[name][index[0]] if len(index) == 1 else (
                        dram[name][index[0], index[1], index[2]] if len(index) == 3 else None)
                    if src is None:
                        if name.startswith(("down", "bdown")):
                            src = dram[name][index[0], :, index[1] * P:index[1] * P + n]
                        else:
                            src = dram[name][index[0], index[1]]
                    dst = raw[s][:, 0:n]
                    SP.do(lambda e, dst=dst, src=src: e.dma_start(dst, src), self.raw_free[s], dma_sem=raw_landed[s])
                    self.read += 1

            def step(self):
                u = self.seen
                kind, name, index, n = plan[u]
                s = u % RAW_SLOTS
                landed = (raw_landed[s], 16 * (u // RAW_SLOTS + 1))
                src = raw[s][:, 0:n]
                if kind == "w":
                    q = self.n_split % SPLIT_SLOTS
                    hi, lo = w_hi[q][:, 0:n], w_lo[q][:, 0:n]
                    t_hi = SC.act(hi, src, ACT.Copy, after=[landed, *self.split_free[q]])
                    t_lo = DVE.tt(lo, src, hi.bitcast(F32), ALU.subtract, after=[landed, t_hi])
                    self.raw_free[s] = [t_hi, t_lo]
                    self.ready.append((name, index, hi, lo, t_lo, q))
                    self.n_split += 1
                else:
                    l, g, kp = index
                    if kp == 0:
                        self.fold(keep=1)
                    a = self.n_groups % 2
                    acc = ada_acc[a]
                    for j in range(2):
                        k = 2 * kp + j
                        w = src[:, j * T:(j + 1) * T]
                        if k == 0:
                            t = DVE.ts(acc[:, :], w, c_act[:, 0:1], None, ALU.mult,
                                       after=[landed, self.c_token, *self.acc_free[a]])
                        else:
                            t = DVE.stt(acc[:, :], w, c_act[:, k:k + 1], acc[:, :], ALU.mult, ALU.add,
                                        after=[landed, self.acc_token])
                        self.acc_token = t
                    self.raw_free[s] = [t]
                    if kp == 3:
                        self.sums.append((l, g, a, t))
                        self.n_groups += 1
                self.seen += 1
                self.load()

            def fold(self, keep=0):
                while len(self.sums) > keep:
                    l, g, a, t = self.sums.pop(0)
                    bank = S.next()
                    for i in range(4):
                        m = PE.mm(bank.buf[:, i:i + 1], ada_acc[a][:, i * P:(i + 1) * P], ones[:, 0:1], True, True,
                                  after=[t, ones_token, *bank.free], signal=(i == 3))
                    v = DVE.tt(mod[:, l, 4 * g:4 * g + 4], bank.buf[:, 0:4], col("ada_b", 48 * l + 4 * g, 4), ALU.add,
                               after=[m, cols_token])
                    self.acc_free[a] = [m]
                    bank.free = [v]
                    self.mod_token[l] = v

            def take(self, name, *index):
                while self.n_split < min(self.taken + 1 + AHEAD, n_w) and self.n_split - self.finished < SPLIT_SLOTS:
                    self.step()
                got = self.ready.pop(0)
                assert (got[0], got[1]) == (name, index), (got[0], got[1], name, index)
                self.taken += 1
                return got

            def done(self, unit, token):
                self.finished += 1
                self.split_free[unit[5]] = [token]

        n_w = sum(p[0] == "w" for p in plan)
        stream = Stream()

        SP.do(lambda e: e.dma_start(cols[:, 0:NCOLS], dram["cols"]), dma_sem=cols_landed)
        cols_token = (cols_landed, 16)
        stream.load()
        SP.do(lambda e: e.dma_start(x[:, :, :], dram["x"]), dma_sem=x_landed)
        x_token = (x_landed, 16)
        GP.memset(mean_d[:, :], 1.0 / D)
        GP.memset(eps, EPS)
        GP.memset(table_probe, 0.5)
        GP.memset(ident[:, :], 0.0)
        ones_token = GP.memset(ones[:, :], 1.0)
        ident_token = GP.do(lambda e: e.affine_select(out=ident[:, :], in_=ident[:, :], compare_op=ALU.not_equal,
                                                      fill=1.0, base=0, pattern=[[-1, P]], channel_multiplier=1),
                            after=[ones_token])
        stream.c_token = SC.act(c_act[:, :], col("c", 0, 8), ACT.Silu, after=[cols_token])
        t = DVE.tt(lb[:, :], col("hg_lb", 0, 8), col("hg_lb", 8, 8), ALU.subtract, after=[cols_token])
        t = SC.act(lb[:, :], lb[:, :], ACT.Sigmoid, after=[t])
        lb_token = DVE.ts(one_m_lb[:, :], lb[:, :], -1.0, 1.0, ALU.mult, ALU.add, after=[t])

        x_ready = [x_token] * KT
        h_ready = [None] * KT
        h_dead = [None]

        def barrier():
            return [lane.last for lane in (PE, DVE, SC, GP)]

        def fm_products(names, src_hi=None, src_lo=None, ready=None, bank=None, k0=0, nk=KT, first=True, last=True,
                        midway=None):
            src_hi, src_lo, ready = (src_hi or h_hi), (src_lo or h_lo), (ready or h_ready)
            units = [stream.take(*n) for n in names]
            banks = [bank or G.next() for _ in names]
            for i in range(nk):
                k = k0 + i
                w = slice(i * P, (i + 1) * P)
                if midway is not None and i == nk - 2:
                    midway()
                for (_, _, hi, lo, split, _), b in zip(units, banks):
                    PE.mm(b.buf, hi[:, w], src_hi[:, k, :], first and i == 0, False,
                          after=[split, ready[k], *(b.free if first and i == 0 else [])])
                    PE.mm(b.buf, hi[:, w], src_lo[:, k, :], False, False)
                    t = PE.mm(b.buf, lo[:, w], src_hi[:, k, :], False, last and i == nk - 1, signal=(i == nk - 1))
            for unit in units:
                stream.done(unit, t)
            if src_hi is h_hi:
                h_dead[0] = t
            stream.fold()
            return [(b, t) for b in banks]

        def fm_product(name, *index, **kw):
            return fm_products([(name, *index)], **kw)[0]

        def tm_product(name, group, evacuate):
            banks = [G.next() for _ in range(4)]
            for kp in range(4):
                unit = stream.take(name, group, kp)
                _, _, hi, lo, split, _ = unit
                for tok in range(4):
                    bank = banks[tok]
                    c = slice(tok * P, (tok + 1) * P)
                    for j in range(2):
                        k = 2 * kp + j
                        w = slice(j * T, (j + 1) * T)
                        PE.mm(bank.buf, h_hi[:, k, c], hi[:, w], k == 0, False,
                              after=[split, h_ready[k], *(bank.free if k == 0 else [])])
                        PE.mm(bank.buf, h_hi[:, k, c], lo[:, w], False, False)
                        t = PE.mm(bank.buf, h_lo[:, k, c], hi[:, w], False, k == KT - 1,
                                  signal=(j == 1 and (kp == 3 or tok == 3)))
                    if kp == 3:
                        evacuate(tok, bank, t)
                stream.done(unit, t)
                h_dead[0] = t
                stream.fold()

        def split_into(hi, lo, k, value, after, readers_done=()):
            t_hi = SC.act(hi[:, k, :], value, ACT.Copy, after=[*after, *readers_done])
            t_lo = DVE.tt(lo[:, k, :], value, hi[:, k, :].bitcast(F32), ALU.subtract, after=[*after, t_hi])
            return t_hi, t_lo

        sq_ring = Ring([hh32[:, 6, :], hh32[:, 7, :]])
        ssum = hh32[:, 5, :]
        rstd = hl32[:, 7, :]
        norm_state = {}

        def square_sum(k):
            slot = sq_ring.next()
            if k < 2:
                slot.free = [h_dead[0], DVE.last]
            t = SC.act(slot.buf, x[:, k, :], ACT.Square, after=[x_ready[k], *slot.free])
            if k == KT - 1:
                norm_state["last"] = (slot, t)
                return
            if k == 0:
                t = GP.ts(ssum, slot.buf, 1.0, None, ALU.mult, after=[t, h_dead[0], DVE.last])
            else:
                t = GP.tt(ssum, ssum, slot.buf, ALU.add, after=[t, norm_state["sum"]])
            norm_state["sum"] = t
            slot.free = [t]

        def inverse_rms(out, bank, n_token, after=()):
            t = SC.act(out, bank.buf, ACT.Ln, bias=eps[:, 0:1], after=[n_token, ones_token, *after])
            bank.free = [t]
            return SC.act(out, out, ACT.Exp, scale=-0.5, after=[t])

        def start_rms():
            bank = norm_state["bank"] = S.next()
            PE.mm(bank.buf, mean_d[:, :], ssum, True, False, after=[norm_state["sum"], ones_token, *bank.free])

        def finish_rms():
            if "bank" not in norm_state:
                start_rms()
            slot, t_last = norm_state["last"]
            bank = norm_state.pop("bank")
            t = PE.mm(bank.buf, mean_d[:, :], slot.buf, False, True, after=[t_last], signal=True)
            return inverse_rms(rstd, bank, t, after=[h_dead[0]])

        def norm_to_h(gain_name, layer=None, which=0, ahead=False):
            t_r = norm_state.pop("rstd", None) or finish_rms()
            if layer is None:
                g, shift, t_g = col(gain_name, 0, 8), None, cols_token
            else:
                t_g = DVE.stt(gain[:, :], mod[:, layer, 24 * which + 8:24 * which + 16], 1.0, col(gain_name, 0, 8),
                              ALU.add, ALU.mult, after=[stream.mod_token[layer], cols_token, DVE.last])
                g, shift = gain, mod[:, layer, 24 * which:24 * which + 8]
            for k in range(KT):
                v = hl32[:, k, :]
                t = DVE.stt(v, x[:, k, :], g[:, k:k + 1], rstd, ALU.mult, ALU.mult,
                            after=[t_r, t_g, x_ready[k], h_dead[0]])
                if shift is None:
                    t_hi = SC.act(h_hi[:, k, :], v, ACT.Copy, after=[t])
                    t = DVE.tt(h_lo[:, k, :], v, h_hi[:, k, :].bitcast(F32), ALU.subtract, after=[t_hi, t])
                else:
                    t_hi = SC.act(h_hi[:, k, :], v, ACT.Identity, bias=shift[:, k:k + 1], after=[t])
                    t = DVE.stt(h_lo[:, k, :], v, shift[:, k:k + 1], h_hi[:, k, :].bitcast(F32), ALU.add, ALU.subtract,
                                after=[t_hi, t])
                h_ready[k] = t
                if ahead and k % 2 == 1 and k < 7:
                    stream.step()

        def load_table(f):
            SC.act(table_probe, ones[:, 0:1], f, after=[ones_token, SC.last])

        def residual(k, bank, token, scale, after=()):
            x_ready[k] = DVE.stt(x[:, k, :], bank.buf, scale, x[:, k, :], ALU.mult, ALU.add,
                                 after=[token, x_ready[k], *after])
            bank.free = [x_ready[k]]
            square_sum(k)

        def normalize_x(gain_name):
            t_r = finish_rms()
            for k in range(KT):
                x_ready[k] = DVE.stt(x[:, k, :], x[:, k, :], col(gain_name, k), rstd, ALU.mult, ALU.mult,
                                     after=[t_r, x_ready[k], cols_token])

        def causal_conv(out, source, w, after, bias=None, free=()):
            if bias is None:
                t = DVE.ts(out, source, w[2], None, ALU.mult, after=[*after, *free])
            else:
                t = DVE.ts(out, source, w[2], bias, ALU.mult, ALU.add, after=[*after, *free])
            t = DVE.stt(out[:, 1:T], source[:, 0:T - 1], w[1], out[:, 1:T], ALU.mult, ALU.add, after=[t])
            return DVE.stt(out[:, 2:T], source[:, 0:T - 2], w[0], out[:, 2:T], ALU.mult, ALU.add, after=[t])

        phase = [0]

        def ffn(up, down, scale, conv=None):
            phase[0] += 1
            start = barrier()
            mid_hi = at(f"mid_hi{phase[0]}", 0, [P, FT, T], F32R)
            mid_lo = at(f"mid_lo{phase[0]}", 44 * KB, [P, FT, T], F32R)
            temps = Ring([at(f"act{phase[0]}_{i}", (88 + 2 * i) * KB, [P, T])[:, :] for i in range(3)], start)
            mid_ready = [None] * FT
            for j in range(FT):
                (a, t_a), (v, t_v) = fm_products([(up, j), (up, FT + j)])
                s = temps.next()
                if conv is not None:
                    wn, bn = conv
                    t = causal_conv(s.buf, a.buf, [col(wn, 22 * i + j) for i in range(3)], [t_a, cols_token],
                                    bias=col(bn, j), free=s.free)
                    a.free = [t]
                    t = SC.act(s.buf, s.buf, ACT.Silu, after=[t])
                else:
                    t = SC.act(s.buf, a.buf, ACT.Silu, after=[t_a, *s.free])
                    a.free = [t]
                t = DVE.tt(s.buf, s.buf, v.buf, ALU.mult, after=[t, t_v])
                v.free = [t]
                t_hi, t_lo = split_into(mid_hi, mid_lo, j, s.buf, [t], start if j == 0 else ())
                s.free = [t_hi, t_lo]
                mid_ready[j] = t_lo
            load_table(ACT.Ln)
            for n in range(KT):
                bank = G.next()
                for k0 in range(0, FT, 8):
                    nk = min(8, FT - k0)
                    last = k0 + nk == FT
                    _, t = fm_product(down, n, k0, src_hi=mid_hi, src_lo=mid_lo, ready=mid_ready, bank=bank,
                                      k0=k0, nk=nk, first=(k0 == 0), last=last,
                                      midway=(start_rms if last and n == KT - 1 else None))
                residual(n, bank, t, scale(n))

        class Head:
            pass

        class Gated:

            def __init__(self, tag, base, dv, block, start):
                self.dv, self.block, self.nb, self.start = dv, block, CHUNK // block, start
                o = [base]

                def take(name, shape, dt=F32):
                    size = int(np.prod(shape[1:])) * 4
                    t = at(f"{tag}_{name}", o[0], shape, dt)
                    o[0] += (size + 31) // 32 * 32
                    return t

                nb = self.nb
                self.kd = Ring([take(f"kd{i}", [P, NCHUNK, nb, CHUNK]) for i in range(2)], start)
                self.qd = Ring([take(f"qd{i}", [P, T]) for i in range(2)], start)
                self.qi = Ring([take(f"qi{i}", [P, T]) for i in range(2)], start)
                self.dec = Ring([take(f"dec{i}", [P, NCHUNK]) for i in range(2)], start)
                self.ks = Ring([take(f"ks{i}", [P, T]) for i in range(2)], start)
                self.kst = Ring([take("kst", [P, 4, P])], start)
                self.st = Ring([take("st", [P, NCHUNK, dv])], start)
                self.sc = Ring([take(f"sc{i}", [P, 4, P]) for i in range(2 if dv == P else 1)], start)
                self.sq = Ring([take(f"sq{i}", [P, T]) for i in range(2)], start)
                self.rstd = Ring([take("rstd", [P, T])], start)
                self.mask = take("mask", [P, 4 * CHUNK], U32)
                self.mean = take("mean", [P, P])
                self.one_reset = take("reset", [P, T])
                self.end = o[0]
                t0 = GP.memset(self.mean[:, :], 1.0 / dv, after=start)
                m = self.mask[:, :]
                mf = self.sc.slots[0].buf[:, :, 0:CHUNK]
                t = GP.memset(mf, 1.0, after=start)
                for half in range(2):
                    v = mf[64 * half:64 * half + 64, :, :]
                    t = GP.do(lambda e, v=v: e.affine_select(out=v, in_=v, compare_op=ALU.is_ge, fill=0.0, base=0,
                                                             pattern=[[0, 4], [1, CHUNK]], channel_multiplier=-1),
                              after=[t])
                t = DVE.copy(m.rearrange("p (c t) -> p c t", t=CHUNK), mf, after=[t])
                for s in self.sc.slots:
                    s.free = [GP.memset(s.buf[:, :, :], 0.0, after=[t, *start])]
                t = GP.memset(self.one_reset[:, :], 1.0, after=start)
                r = self.one_reset[:, :].rearrange("p (c s) -> p c s", s=CHUNK)
                self.const = GP.memset(r[:, :, 0:1], 0.0, after=[t])

            def running_sum(self, out, logs, after):
                return DVE.do(lambda e: e.tensor_tensor_scan(out, self.one_reset[:, :], logs, 0.0, ALU.mult, ALU.add),
                              after=[self.const, *after])

            def exponents(self, b, t_b):
                bs, nb = self.block, self.nb
                n = Head()
                n.kd, n.qd, n.qi, n.dec, n.ks = (r.next() for r in (self.kd, self.qd, self.qi, self.dec, self.ks))
                blocks = b.rearrange("p (n s) -> p n s", s=bs)
                chunks = b.rearrange("p (c s) -> p c s", s=CHUNK)
                ref = blocks[:, :, bs // 2 - 1:bs // 2]
                t2 = DVE.tt(n.qd.buf[:, :].rearrange("p (n s) -> p n s", s=bs), blocks,
                            ref.to_broadcast([P, T // bs, bs]), ALU.subtract, after=[t_b, *n.qd.free])
                for_blocks = b.rearrange("p (c j s) -> p c j s", j=nb, s=bs)[:, :, :, bs // 2 - 1:bs // 2]
                kv4 = n.kd.buf[:, :, :, :]
                t1 = DVE.tt(kv4, for_blocks.to_broadcast([P, NCHUNK, nb, CHUNK]),
                            chunks.unsqueeze(2).to_broadcast([P, NCHUNK, nb, CHUNK]), ALU.subtract,
                            after=[t_b, *n.kd.free])
                t3 = GP.tt(n.ks.buf[:, :].rearrange("p (c s) -> p c s", s=CHUNK),
                           chunks[:, :, CHUNK - 1:CHUNK].to_broadcast([P, NCHUNK, CHUNK]), chunks, ALU.subtract,
                           after=[t_b, *n.ks.free])
                if nb > 1:
                    t1 = GP.do(lambda e: e.affine_select(out=kv4, in_=kv4, compare_op=ALU.is_ge, fill=-1.0e4,
                                                         base=bs - 1, pattern=[[0, NCHUNK], [bs, nb], [-1, CHUNK]],
                                                         channel_multiplier=0), [t1])
                n.b, n.t_b, n.t_kd, n.t_qd, n.t_ks = b, t_b, t1, t2, t3
                return n

            def exponentials(self, n):
                subtracted = [n.t_kd, n.t_qd, n.t_ks]
                n.t_qd = SC.act(n.qd.buf[:, :], n.qd.buf[:, :], ACT.Exp, after=[n.t_qd])
                n.t_ks = SC.act(n.ks.buf[:, :], n.ks.buf[:, :], ACT.Exp, after=[n.t_ks])
                n.t_qi = SC.act(n.qi.buf[:, :], n.b, ACT.Exp, after=[n.t_b, *n.qi.free])
                flat = n.kd.buf[:, :, :, :].rearrange("p c j s -> p (c j s)")
                n.t_kd = SC.act(flat, flat, ACT.Exp, after=[n.t_kd])
                n.b_read = [*subtracted, n.t_qi]

            def weigh(self, n, q, t_q, k, t_k):
                nb = self.nb
                k4 = k.rearrange("p (c s) -> p c s", s=CHUNK).unsqueeze(2).to_broadcast([P, NCHUNK, nb, CHUNK])
                kv4 = n.kd.buf[:, :, :, :]
                ends_ = n.qi.buf[:, :].rearrange("p (c s) -> p c s", s=CHUNK)[:, :, CHUNK - 1:CHUNK]
                n.t_dec = DVE.copy(n.dec.buf[:, :].unsqueeze(2), ends_, after=[n.t_qi, *n.dec.free])
                n.t_ks = GP.tt(n.ks.buf[:, :], n.ks.buf[:, :], k, ALU.mult, after=[n.t_ks, t_k])
                n.t_kd = DVE.tt(kv4, kv4, k4, ALU.mult, after=[n.t_kd, t_k])
                n.t_qd = DVE.tt(n.qd.buf[:, :], n.qd.buf[:, :], q, ALU.mult, after=[n.t_qd, t_q])
                n.t_qi = GP.tt(n.qi.buf[:, :], n.qi.buf[:, :], q, ALU.mult, after=[n.t_qi, t_q, n.t_dec])
                n.inputs_read = [n.t_kd, n.t_ks, n.t_qd, n.t_qi]

            def scores(self, n):
                bs, nb = self.block, self.nb
                bank = S.next()
                first = [n.t_kd, n.t_qd, *bank.free]
                for c in range(NCHUNK):
                    half = slice(64 * (c % 2), 64 * (c % 2) + 64)
                    for j in range(nb):
                        a = (c // 2) * CHUNK + j * bs
                        t_sc = PE.mm(bank.buf[half, a:a + bs], n.kd.buf[:, c, j, :],
                                     n.qd.buf[:, c * CHUNK + j * bs:c * CHUNK + (j + 1) * bs],
                                     True, True, after=first, signal=(c == NCHUNK - 1 and j == nb - 1))
                        first = []
                n.kd.free, n.qd.free = [t_sc], [t_sc]
                n.sc = self.sc.next()
                for i in range(2):
                    half = slice(64 * i, 64 * i + 64)
                    to = n.sc.buf[half, :, half]
                    mask, scores = (a[half, 0:4 * CHUNK].rearrange("p (c t) -> p c t", t=CHUNK)
                                    for a in (self.mask, bank.buf))
                    n.t_m = DVE.do(lambda e, to=to, mask=mask, scores=scores: e.copy_predicated(to, mask, scores),
                                   after=[t_sc, *n.sc.free])
                bank.free = [n.t_m]
                bank = S.next()
                for i in range(4):
                    t = PE.tr(bank.buf[:, i * P:(i + 1) * P], n.ks.buf[:, i * P:(i + 1) * P], ident[:, :],
                              after=[n.t_ks, ident_token, *bank.free], signal=(i == 3))
                n.ks.free = [t]
                n.kst = self.kst.next()
                n.t_kst = SC.act(n.kst.buf[:, :, :].rearrange("p a b -> p (a b)"), bank.buf, ACT.Copy,
                                 after=[t, *n.kst.free])
                bank.free = [n.t_kst]

            def states(self, n, v_tm, t_v, v0):
                dv = self.dv
                n.st = self.st.next()
                per = 2 * (T // dv)
                for c0 in range(0, NCHUNK - 1, per):
                    banks = [S.next(), S.next()]
                    group = range(c0, min(c0 + per, NCHUNK - 1))
                    places = [banks[c % 2].buf[:, (c - c0) // 2 * dv:(c - c0) // 2 * dv + dv] for c in group]
                    for c, place in zip(group, places):
                        half = slice(64 * (c % 2), 64 * (c % 2) + 64)
                        t = PE.mm(place, n.kst.buf[half, c // 2, :], v_tm[half, c // 2, v0:v0 + dv], True, True,
                                  after=[n.t_kst, t_v, *banks[c % 2].free], signal=(c == group[-1]))
                    for c, place in zip(group, places):
                        if c == 0:
                            t_st = DVE.copy(n.st.buf[:, 1, :], place, after=[t, *n.st.free])
                        else:
                            t_st = DVE.stt(n.st.buf[:, c + 1, :], n.st.buf[:, c, :], n.dec.buf[:, c:c + 1], place,
                                           ALU.mult, ALU.add, after=[t, t_st, n.t_dec])
                    banks[0].free = banks[1].free = [t_st]
                n.kst.free, n.dec.free, n.t_st = [t], [t_st], t_st

            def output(self, n, d, v_tm, t_v, v0):
                o = O.next()
                first = [n.t_m, n.t_st, n.t_qi, t_v, *o.free]
                for i in range(4):
                    PE.mm(o.buf[:, i * P:(i + 1) * P], v_tm[:, i, v0 + d * P:v0 + (d + 1) * P], n.sc.buf[:, i, :],
                          True, False, after=first)
                    for c in range(max(2 * i, 1), 2 * i + 2):
                        cs = slice(c * CHUNK, (c + 1) * CHUNK)
                        t = PE.mm(o.buf[:, cs], n.st.buf[:, c, d * P:(d + 1) * P], n.qi.buf[:, cs], False,
                                  c == 2 * i + 1, signal=(c == NCHUNK - 1))
                if d == self.dv // P - 1:
                    n.sc.free, n.st.free, n.qi.free = [t], [t], [t]
                return o, t

        for k in range(KT):
            square_sum(k)
        while stream.seen < 17:
            stream.step()
            if stream.seen == 12:
                norm_state["rstd"] = finish_rms()
        stream.fold()
        norm_to_h("norm_mix0", 0, 0, ahead=True)

        phase_start = barrier()
        o_all = at("hg_o", 0, [P, 8, T])
        v_tm = at("hg_v_tm", 16 * KB, [P, 4, D])
        gated = Gated("hg", 32 * KB, P, 16, phase_start)
        b_sb = Ring([at(f"hg_b{i}", gated.end + 2 * KB * i, [P, T]) for i in range(2)], phase_start)
        k_sb = Ring([at(f"hg_k{i}", gated.end + 2 * KB * (2 + i), [P, T]) for i in range(2)], phase_start)
        q_sb = Ring([at("hg_q", gated.end + 8 * KB, [P, T])], phase_start)
        g_sb = Ring([at(f"hg_g{i}", gated.end + 2 * KB * (5 + i), [P, T]) for i in range(3)], phase_start)
        v_done = [None]
        for g in range(2):
            def put(tok, bank, t, g=g):
                v_done[0] = SC.act(v_tm[:, tok, g * T:(g + 1) * T], bank.buf, ACT.Copy, after=[t, *phase_start])
                bank.free = [v_done[0]]
            tm_product("hg_v", g, put)
        o_ready = [None] * 8

        def mean_square(n):
            n.mean_bank = S.next()
            n.t_mean = PE.mm(n.mean_bank.buf, gated.mean[:, :], n.sq.buf[:, :], True, True,
                             after=[n.t_sq, gated.const, *n.mean_bank.free], signal=True)
            n.sq.free = [n.t_mean]

        def head_norm(n, h):
            r = gated.rstd.next()
            t = inverse_rms(r.buf[:, :], n.mean_bank, n.t_mean, after=r.free)
            t = DVE.stt(o_all[:, h, :], n.o.buf, col("gnorm"), r.buf[:, :], ALU.mult, ALU.mult,
                        after=[t, n.t_sq, cols_token, *phase_start])
            n.o.free = [t]
            r.free = [t]
            o_ready[h] = DVE.tt(o_all[:, h, :], o_all[:, h, :], n.g.buf[:, :], ALU.mult, after=[t, n.t_g])
            n.g.free = [o_ready[h]]

        older = last = None
        for h in range(10):
            n = None
            if last is not None:
                gated.scores(last)
            if h < 8:
                bank, t = fm_product("hg_f", h)
                b, k, sq = b_sb.next(), k_sb.next(), gated.sq.next()
                t1 = SC.act(sq.buf[:, :], bank.buf, ACT.Sigmoid, after=[t, *sq.free])
                t2 = SC.act(k.buf[:, :], bank.buf, ACT.Sigmoid, scale=-1.0, after=[t, *k.free])
                bank.free = [t2]
            if last is not None:
                last.g = g_sb.next()
                t = SC.act(last.g.buf[:, :], last.g_bank.buf, ACT.Sigmoid, after=[last.t_g, *last.g.free])
                last.t_g = DVE.tt(last.g.buf[:, :], last.g.buf[:, :], last.g_bank.buf, ALU.mult, after=[t, last.t_g])
                last.g_bank.free = [last.t_g]
            if h < 8:
                t_k = DVE.ts(k.buf[:, :], k.buf[:, :], one_m_lb[:, h:h + 1], None, ALU.mult, after=[t2, lb_token])
                t = SC.act(sq.buf[:, :], sq.buf[:, :], ACT.Ln, scale=one_m_lb[:, h:h + 1], bias=lb[:, h:h + 1],
                           after=[t1, lb_token])
                t_b = gated.running_sum(b.buf[:, :], sq.buf[:, :], [t, *b.free])
                sq.free = [t_b]
                n = gated.exponents(b.buf[:, :], t_b)
            if older is not None:
                mean_square(older)
                head_norm(older, h - 2)
            if last is not None:
                gated.states(last, v_tm, v_done[0], (h - 1) * P)
            if n is not None:
                bank, t = fm_product("hg_q", h)
                q = q_sb.next()
                t_q = SC.act(q.buf[:, :], bank.buf, ACT.Copy, after=[t, *q.free])
                bank.free = [t_q]
                gated.exponentials(n)
                b.free = n.b_read
            if last is not None:
                last.o, t = gated.output(last, 0, v_tm, v_done[0], (h - 1) * P)
                last.sq = gated.sq.next()
                last.t_sq = SC.act(last.sq.buf[:, :], last.o.buf, ACT.Square, after=[t, *last.sq.free])
            if n is not None:
                gated.weigh(n, q.buf[:, :], t_q, k.buf[:, :], t_k)
                q.free = k.free = n.inputs_read
                n.g_bank, n.t_g = fm_product("hg_g", h)
            older, last = last, n
        start = barrier()
        on_hi = at("hg_on_hi", 16 * KB, [P, 8, T], F32R)
        on_lo = at("hg_on_lo", 32 * KB, [P, 8, T], F32R)
        on_ready = [split_into(on_hi, on_lo, h, o_all[:, h, :], [o_ready[h]], start if h == 0 else ())[1] for h in range(8)]
        for n in range(KT):
            bank, t = fm_product("hg_out", n, src_hi=on_hi, src_lo=on_lo, ready=on_ready,
                                 midway=(start_rms if n == KT - 1 else None))
            residual(n, bank, t, mod[:, 0, 16 + n:17 + n], [stream.mod_token[0]])
        norm_to_h("norm_ffn0", 0, 1)
        ffn("up0", "down0", lambda n: mod[:, 0, 40 + n:41 + n], ("conv_w0", "conv_b0"))
        stream.fold()
        norm_to_h("norm_mix1", 1, 0)

        phase_start = barrier()
        o_all = at("nsa_o", 0, [P, 8, T])
        v2 = at("nsa_v2", 16 * KB, [P, 4, 8, 2, HD], F32R)
        k2 = at("nsa_k2", 32 * KB, [P, 2, 2, 2, T], F32R)
        cw1 = at("cmp_w1", 48 * KB, [P, 2, CMP_LEN, HD])
        kv_c = at("cmp_kv", 64 * KB, [P, 4, T])
        probs = Ring([at(f"probs{i}", (48 + 5 * i) * KB, [P, 1280]) for i in range(3)])
        probs_t = [Ring([(at(f"probs_t_hi{b}", (63 + 2 * b) * KB, [P, T], F32R),
                          at(f"probs_t_lo{b}", (68 + 2 * b) * KB, [P, T], F32R))]) for b in range(2)]
        probs_t.append(Ring([(at("probs_t_hi2", 67 * KB, [P, T // 2], F32R), at("probs_t_lo2", 72 * KB, [P, T // 2], F32R))]))
        q_sb = Ring([at(f"nsa_q{i}", (73 + 2 * i) * KB, [P, T], F32R) for i in range(3)], phase_start)
        bias_h = Ring([at(f"bias{i}", (79 + 2 * i) * KB, [P, T]) for i in range(2)], phase_start)
        dist = at("dist", 83 * KB, [P, T])
        pc_t = Ring([(at("pc_t_hi", 85 * KB, [NCMP, T], F32R), at("pc_t_lo", 87 * KB, [NCMP, T], F32R))], phase_start)
        o_low = Ring([at("o_low", 89 * KB, [P, T])], phase_start)
        small = [91 * KB]

        def little(name, shape, dt=F32):
            t = at(f"nsa_{name}", small[0], shape, dt)
            small[0] += (int(np.prod(shape[1:])) * 4 + 31) // 32 * 32
            return t

        dist_c = little("dist_c", [P, 4, NCMP])
        pc = Ring([little(f"pc{i}", [P, 4, NCMP]) for i in range(2)], phase_start)
        gate = little("gate", [P, 4, 48])
        valid0 = little("valid0", [P, 1])
        cw2 = little("cmp_w2", [HD, 2, HD])
        z = little("z", [HD, 2, 2, 2, NCMP])
        pe_bias = little("pe_bias", [HD, 2])
        NC2 = NCMP + NCMP % 2
        kc2_hi = little("kc2_hi", [P, 2, 2, NC2], F32R)
        kc2_lo = little("kc2_lo", [P, 2, 2, NC2], F32R)
        vc2 = little("vc2", [NCMP, NSA_GROUPS, 2, HD], F32R)
        maxes = Ring([little(f"maxes{i}", [P, 3, 4]) for i in range(2)], phase_start)
        sums = Ring([little(f"sums{i}", [P, 3, 4]) for i in range(2)], phase_start)

        for half in range(2):
            SP.do(lambda e, half=half: e.dma_start(cw1[64 * half:64 * half + 64, :, :, :], dram["cmp_w1"]),
                  phase_start, dma_sem=cmp_landed)
        SP.do(lambda e: e.dma_start(cw2[:, :, :], dram["cmp_w2"]), phase_start, dma_sem=cmp_landed)
        cmp_token = (cmp_landed, 48)

        t = GP.do(lambda e: e.iota(dist[:, :], pattern=[[-1, T]], base=384, channel_multiplier=1,
                                   allow_small_or_imprecise_dtypes=True), phase_start)
        dist_token = GP.do(lambda e: e.affine_select(out=dist[:, :], in_=dist[:, :], compare_op=ALU.is_ge, fill=MASKED,
                                                     base=384, pattern=[[-1, T]], channel_multiplier=1), [t])
        t = GP.do(lambda e: e.iota(dist_c[:, :, :], pattern=[[P, 4], [-CMP_STRIDE, NCMP]], base=0, channel_multiplier=1,
                                   allow_small_or_imprecise_dtypes=True), phase_start)
        t = GP.ts(dist_c[:, :, :], dist_c[:, :, :], -(CMP_LEN - 1) / 2.0, None, ALU.add, after=[t])
        distc_token = GP.do(lambda e: e.affine_select(out=dist_c[:, :, :], in_=dist_c[:, :, :], compare_op=ALU.is_ge,
                                                      fill=MASKED, base=-(CMP_LEN - 1),
                                                      pattern=[[P, 4], [-CMP_STRIDE, NCMP]], channel_multiplier=1), [t])
        t = GP.memset(valid0[:, :], 1.0, after=phase_start)
        valid_token = GP.do(lambda e: e.affine_select(out=valid0[:, :], in_=valid0[:, :], compare_op=ALU.is_ge, fill=0.0,
                                                      base=-(CMP_LEN - 1), pattern=[[0, 1]], channel_multiplier=1), [t])

        v_done = [None]

        def put_v(tok, bank, t):
            src = bank.buf.rearrange("p (g d) -> p g d", d=HD)
            t = SC.act(v2[:, tok, :, 0, :], src, ACT.Copy, after=[t, *phase_start])
            v_done[0] = DVE.tt(v2[:, tok, :, 1, :], src, v2[:, tok, :, 0, :].bitcast(F32), ALU.subtract, after=[t])
            bank.free = [v_done[0]]

        tm_product("nsa_v", 0, put_v)
        unit = stream.take("nsa_gate", 0)
        bank = G.next()
        for tok in range(4):
            c = slice(tok * P, (tok + 1) * P)
            for k in range(KT):
                w = slice(48 * k, 48 * k + 48)
                out = bank.buf[:, 48 * tok:48 * tok + 48]
                PE.mm(out, h_hi[:, k, c], unit[2][:, w], k == 0, False, after=[unit[4], *bank.free])
                PE.mm(out, h_hi[:, k, c], unit[3][:, w], False, False)
                t = PE.mm(out, h_lo[:, k, c], unit[2][:, w], False, k == KT - 1, signal=(k == KT - 1))
        stream.done(unit, t)
        t = SC.act(gate[:, :, :].rearrange("p a b -> p (a b)"), bank.buf[:, 0:192], ACT.Sigmoid, after=[t, *phase_start])
        bank.free = [t]
        g0 = gate[:, 0, :].rearrange("p (h b) -> p h b", b=3)[:, :, 0:1]
        gate_token = DVE.ts(g0, g0, valid0[:, 0:1], None, ALU.mult, after=[t, valid_token])

        def stack_keys(tile, bank, t, free):
            br = (tile - 4) // 2
            for par in range(2):
                src = bank.buf[64 * par:64 * par + 64, :]
                for rows in (slice(0, 64), slice(64, P)):
                    t_hi = SC.act(k2[rows, par, br, 0, :], src, ACT.Copy, after=[t, *free])
                for rows in (slice(0, 64), slice(64, P)):
                    t = DVE.tt(k2[rows, par, br, 1, :], src, k2[rows, par, br, 0, :].bitcast(F32), ALU.subtract,
                               after=[t, t_hi])
            bank.free = [t]
            return t

        def stack_queries(bank, t):
            out = []
            for half in range(2):
                q = q_sb.next()
                src = bank.buf[64 * half:64 * half + 64, :]
                t_hi = SC.act(q.buf[0:64, :], src, ACT.Copy, after=[t, *q.free])
                t = DVE.tt(q.buf[64:P, :], src, q.buf[0:64, :].bitcast(F32), ALU.subtract, after=[t, t_hi])
                out.append((q, t))
            bank.free = [t]
            return out

        for i in (0, 1, 2, 3, 4, 6):
            bank, t = fm_product("nsa_kv", i)
            if i >= 4:
                t_kv = stack_keys(i, bank, t, phase_start)
                continue
            t_kvc = SC.act(kv_c[:, i, :], bank.buf, ACT.Copy, after=[t, *phase_start])
            bank.free = [t_kvc]
            if i == 3:
                zb = [S.next(), S.next()]
                pb = S.next()
                for kv in range(2):
                    for l in range(CMP_LEN):
                        t_pe = PE.mm(pb.buf[0:HD, kv:kv + 1], cw1[0:HD, kv, l, :], col("pe", 32 * kv + l)[0:HD, :],
                                     l == 0, l == CMP_LEN - 1, after=[cmp_token, cols_token, *pb.free],
                                     signal=(l == CMP_LEN - 1))
                t_pe = DVE.copy(pe_bias[:, :], pb.buf[0:HD, 0:2], after=[t_pe, *phase_start])
                pb.free = [t_pe]
                for kv in range(2):
                    for par in range(2):
                        rows = slice(64 * par, 64 * par + 64)
                        a = kv * 2 * NCMP
                        for l in range(CMP_LEN):
                            rhs = kv_c[rows, 2 * kv:2 * kv + 2, l:l + CMP_STRIDE * (NCMP - 1) + 1:CMP_STRIDE]
                            t = PE.mm(zb[par].buf[0:HD, a:a + 2 * NCMP].rearrange("p (a b) -> p a b", a=2), cw1[rows, kv, l, :], rhs,
                                      l == 0, l == CMP_LEN - 1, after=[t_kvc, *zb[par].free], signal=(l == CMP_LEN - 1))
                for kv in range(2):
                    a = kv * 2 * NCMP
                    for par in range(2):
                        t = SC.act(z[:, kv, par, :, :].rearrange("p b n -> p (b n)"), zb[par].buf[0:HD, a:a + 2 * NCMP],
                                   ACT.Silu, bias=pe_bias[:, kv:kv + 1], after=[t, t_pe, *phase_start])
                zb[0].free = zb[1].free = [t]
                t_z = t
                kb = S.next()
                t_0 = GP.memset(kc2_hi[:, :, :, :].bitcast(F32), 0.0, after=phase_start)
                t_0 = GP.memset(kc2_lo[:, :, :, :].bitcast(F32), 0.0, after=phase_start)
                t = PE.mm(kb.buf[0:HD, 0:4 * NCMP], cw2[:, 0, :], z[:, 0, :, :, :].rearrange("p a b n -> p (a b n)"),
                          True, True, after=[t_z, *kb.free], signal=True)
                src = kb.buf[0:HD, 0:4 * NCMP].rearrange("p (g n) -> p g n", n=NCMP)
                for rows in (slice(0, 64), slice(64, P)):
                    to_hi, to_lo = (a[rows, :, :, :].rearrange("p a b n -> p (a b) n")[:, :, 0:NCMP] for a in (kc2_hi, kc2_lo))
                    t1 = SC.act(to_hi, src, ACT.Copy, after=[t, t_0])
                    t_kc = DVE.tt(to_lo, src, to_hi.bitcast(F32), ALU.subtract, after=[t, t1, t_0])
                    t = t_kc
                kb.free = [t_kc]
                vb = S.next()
                for g in range(NSA_GROUPS):
                    t = PE.mm(vb.buf[0:NCMP, HD * g:HD * g + HD], z[:, 1, g % 2, g // 2, :], cw2[:, 1, :], True, True,
                              after=[t_z, *vb.free], signal=True)
                src = vb.buf[0:NCMP, 0:4 * HD].rearrange("p (g d) -> p g d", d=HD)
                t = SC.act(vc2[:, :, 0, :], src, ACT.Copy, after=[t, *phase_start])
                t_vc = DVE.tt(vc2[:, :, 1, :], src, vc2[:, :, 0, :].bitcast(F32), ALU.subtract, after=[t])
                vb.free = [t_vc]
                compressed = barrier()
                for r in (probs, *probs_t):
                    for s in r.slots:
                        s.free = list(compressed)

        OFF_Q = [0, 128, 384, 768]
        scale = HD ** -0.5

        def begin_head(head, pair, half, q, t_q):
            n = Head()
            n.head, n.pair, n.half, n.q, n.t_q = head, pair, half, q, t_q
            n.par, n.gp = (head // 4) % 2, head // 8
            slope = 2.0 ** (-8.0 * (head + 1) / NSA_HEADS)
            n.mx, n.sm, n.c, n.bias = maxes.next(), sums.next(), pc.next(), bias_h.next()
            n.pr, n.t_sum = [], []
            n.t_bias = GP.ts(n.bias.buf[:, :], dist[:, :], -slope / scale, None, ALU.mult, after=[dist_token, *n.bias.free])
            bank = S.next()
            for i in range(4):
                out = bank.buf[:, NC2 * i:NC2 * (i + 1)]
                lhs = q.buf[:, i * P:(i + 1) * P]
                PE.mm(out, lhs, kc2_hi[:, n.par, n.gp, :], True, False, after=[t_q, t_kc, *bank.free])
                t = PE.mm(out, lhs, kc2_lo[:, n.par, n.gp, :], False, True, signal=(i == 3))
            cb = n.c.buf[:, :, :]
            t = DVE.stt(cb, dist_c[:, :, :], -slope / scale,
                        bank.buf[:, 0:4 * NC2].rearrange("p (a n) -> p a n", n=NC2)[:, :, 0:NCMP],
                        ALU.mult, ALU.add, after=[t, distc_token, *n.c.free])
            bank.free = [t]
            m = n.mx.buf[:, 0, :]
            t = DVE.do(lambda e: e.tensor_reduce(m, cb, AX.X, ALU.max), after=[t, *n.mx.free])
            t = DVE.tt(cb, cb, m.unsqueeze(2).to_broadcast([P, 4, NCMP]), ALU.subtract, after=[t])
            n.t_pc = SC.act(cb, cb, ACT.Exp, scale=scale, after=[t])
            return n

        def in_turn(*steps):
            steps = list(steps)
            while steps:
                for s in list(steps):
                    if next(s, steps) is steps:
                        steps.remove(s)

        def branch_scores(n, br):
            p = probs.next()
            for i in range(4):
                w = (i + 1) * P
                bank = S.next()
                lhs = n.q.buf[:, i * P:(i + 1) * P]
                PE.mm(bank.buf[:, 0:w], lhs, k2[:, n.par, br, 0, 0:w], True, False, after=[n.t_q, t_kv, *bank.free])
                t = PE.mm(bank.buf[:, 0:w], lhs, k2[:, n.par, br, 1, 0:w], False, True, signal=True)
                dst, src = p.buf[:, OFF_Q[i]:OFF_Q[i] + w], bank.buf[:, 0:w]
                b, m = n.bias.buf[:, 384 - P * i:T], n.mx.buf[:, 1 + br, i:i + 1]
                t_max = DVE.do(lambda e, dst=dst, src=src, b=b, m=m: e.tensor_tensor_reduce(
                    dst, src, b, -scale, 3.0e38, ALU.add, ALU.min, m), after=[t, n.t_bias, *p.free, *n.mx.free])
                bank.free = [t_max]
                n.t_scored = t
                t_sum = SC.act(dst, dst, ACT.Exp, scale=-1.0, bias=m, accum_out=n.sm.buf[:, 1 + br, i:i + 1],
                               after=[t_max, *n.sm.free])
                yield
            n.pr.append(p)
            n.t_sum.append(t_sum)
            if br == 1:
                n.bias.free = [t_max]
                n.q.free = [n.t_scored]

        def gate_head(n):
            cb = n.c.buf[:, :, :]
            s0 = n.sm.buf[:, 0, :]
            t = DVE.do(lambda e: e.tensor_reduce(s0, cb, AX.X, ALU.add), after=[n.t_pc, *n.sm.free])
            sv = n.sm.buf[:, :, :].rearrange("p a b -> p (a b)")
            t = DVE.do(lambda e: e.reciprocal(sv, sv), after=[t, *n.t_sum])
            gv = gate[:, :, 3 * n.head:3 * n.head + 3].rearrange("p i b -> p b i")
            t_f = DVE.tt(n.sm.buf[:, :, :], n.sm.buf[:, :, :], gv, ALU.mult, after=[t, gate_token])
            n.t_pc = DVE.tt(cb, cb, n.sm.buf[:, 0, :].unsqueeze(2).to_broadcast([P, 4, NCMP]), ALU.mult, after=[t_f])
            n.t_gate, n.t_p = t_f, [None, None]

        def gate_branch(n, br):
            for i in range(4):
                dst = n.pr[br].buf[:, OFF_Q[i]:OFF_Q[i] + (i + 1) * P]
                t = (DVE, GP)[br].ts(dst, dst, n.sm.buf[:, 1 + br, i:i + 1], None, ALU.mult, after=[n.t_gate])
            n.t_p[br] = t
            if br == 1:
                n.mx.free = n.sm.free = [t, n.t_pc]

        def compressed_values(n):
            bank = S.next()
            for i in range(4):
                t = PE.tr(bank.buf[0:NCMP, i * P:(i + 1) * P], n.c.buf[:, i, :], ident[:, :],
                          after=[n.t_pc, ident_token, *bank.free], signal=(i == 3))
            n.c.free = [t]
            pt = pc_t.next()
            hi, lo = pt.buf
            src = bank.buf[0:NCMP, :]
            t_hi = SC.act(hi[:, :], src, ACT.Copy, after=[t, *pt.free])
            t_lo = DVE.tt(lo[:, :], src, hi[:, :].bitcast(F32), ALU.subtract, after=[t, t_hi])
            bank.free = [t_lo]
            n.late = (pt, t_lo)

        def branch_transposes(n, br):
            p, t_p = n.pr[br], n.t_p[br]
            n.pt, n.ready = [r.next() for r in probs_t], []
            for pt, tiles, w in zip(n.pt, BANK_TILES, BANK_WIDTH):
                bank = G.next()
                for j in tiles:
                    for i in range(j, 4):
                        src = p.buf[:, OFF_Q[i] + j * P:OFF_Q[i] + (j + 1) * P]
                        a = PLACE[j][1] + (i - j) * P
                        t = PE.tr(bank.buf[:, a:a + P], src, ident[:, :], after=[t_p, *bank.free], signal=(i == 3))
                hi, lo = (v[:, 0:w] for v in pt.buf)
                src = bank.buf[:, 0:w]
                t_hi = SC.act(hi, src, ACT.Copy, after=[t, *pt.free])
                bank.free = [DVE.tt(lo, src, hi.bitcast(F32), ALU.subtract, after=[t, t_hi])]
                n.ready.append(bank.free[0])
                yield
            p.free = [t]

        def branch_values(n, br):
            g = 2 * n.gp + n.par
            if br == 0:
                n.o = O.next()
                pt, t = n.late
                v = vc2[:, g, :, :].rearrange("p a d -> p (a d)")
                PE.mm(n.o.buf, v, pt.buf[0][:, :], True, False, after=[t, t_vc, *n.o.free])
                t = PE.mm(n.o.buf, v, pt.buf[1][:, :], False, False, signal=True)
                pt.free = [t]
                yield
            for pt, ready, tiles in zip(n.pt, n.ready, BANK_TILES):
                hi, lo = pt.buf
                for j in tiles:
                    w, a = T - j * P, PLACE[j][1]
                    v = v2[:, j, 4 * br + g, :, :].rearrange("p a d -> p (a d)")
                    PE.mm(n.o.buf[:, j * P:T], v, hi[:, a:a + w], False, False, after=[ready, v_done[0]])
                    t = PE.mm(n.o.buf[:, j * P:T], v, lo[:, a:a + w], False, br == 1 and j == 2, signal=(j == tiles[-1]))
                pt.free = [t]
                yield
            if br == 1:
                low = o_low.next()
                t1 = SC.act(low.buf[0:64, :], n.o.buf[64:P, :], ACT.Copy, after=[t, *low.free])
                nsa_o_ready[n.pair] = DVE.tt(o_all[64 * n.half:64 * n.half + 64, n.pair, :], n.o.buf[0:64, :], low.buf[0:64, :],
                                             ALU.add, after=[t, t1, *phase_start])
                n.o.free = low.free = [nsa_o_ready[n.pair]]

        PLACE = {0: (0, 0), 1: (1, 0), 3: (1, 384), 2: (2, 0)}
        BANK_TILES, BANK_WIDTH = ((0,), (1, 3), (2,)), (512, 512, 256)
        nsa_o_ready = [None] * 8
        heads = [(pair, half, 4 * (2 * (pair // 4) + half) + pair % 4) for pair in range(8) for half in range(2)]
        older = last = None
        for step in range(18):
            n = None
            if last is not None:
                gate_head(last)
            if step < 16:
                pair, half, head = heads[step]
                if half == 0:
                    if pair == 4:
                        free = [last.t_scored]
                        for i in (5, 7):
                            bank, t = fm_product("nsa_kv", i)
                            t_kv = stack_keys(i, bank, t, free)
                    bank, t = fm_product("nsa_q", pair)
                    queries = stack_queries(bank, t)
                n = begin_head(head, pair, half, *queries[half])
            if last is not None:
                gate_branch(last, 0)
                gate_branch(last, 1)
            in_turn(*([branch_scores(n, 0)] if n else []), *([branch_values(older, 1)] if older else []))
            if last is not None:
                compressed_values(last)
                in_turn(branch_transposes(last, 0))
            in_turn(*([branch_scores(n, 1)] if n else []), *([branch_values(last, 0)] if last else []))
            if last is not None:
                in_turn(branch_transposes(last, 1))
            older, last = last, n
        start = barrier()
        o_hi = at("nsa_o_hi", 32 * KB, [P, 8, T], F32R)
        o_lo = at("nsa_o_lo", 48 * KB, [P, 8, T], F32R)
        nsa_ready = [split_into(o_hi, o_lo, i, o_all[:, i, :], [nsa_o_ready[i]], start if i == 0 else ())[1] for i in range(8)]
        for n in range(KT):
            bank, t = fm_product("nsa_out", n, src_hi=o_hi, src_lo=o_lo, ready=nsa_ready,
                                 midway=(start_rms if n == KT - 1 else None))
            residual(n, bank, t, mod[:, 1, 16 + n:17 + n], [stream.mod_token[1]])
        norm_to_h("norm_ffn1", 1, 1)
        ffn("up1", "down1", lambda n: mod[:, 1, 40 + n:41 + n], ("conv_w1", "conv_b1"))
        normalize_x("final_norm")

        h_dead[0] = PE.last
        for k in range(KT):
            square_sum(k)
        norm_to_h("b_norm_ffn1")
        ffn("bup1", "bdown1", lambda n: 0.5)
        norm_to_h("b_norm_mix")

        phase_start = barrier()
        merged = at("merged", 0, [P, 8, T])
        c_hi = at("c_hi", 32 * KB, [P, 8, T], F32R)
        c_lo = at("c_lo", 48 * KB, [P, 8, T], F32R)
        temps = Ring([at(f"conv_a{i}", (64 + 2 * i) * KB, [P, T])[:, :] for i in range(3)], phase_start)
        temps2 = Ring([at(f"conv_b{i}", (70 + 2 * i) * KB, [P, T])[:, :] for i in range(3)], phase_start)
        c_ready = [None] * 8
        for i in range(8):
            cc, t_cc = fm_product("b_conv", 8 + i)
            cu, t_cu = fm_product("b_conv", 16 + i)
            cb, t_cb = fm_product("b_conv", i)
            a, y = temps.next(), temps2.next()
            t = SC.act(a.buf, cc.buf, ACT.Copy, after=[t_cc, *a.free])
            cc.free = [t]
            t = DVE.tt(a.buf, a.buf, cu.buf, ALU.mult, after=[t, t_cu])
            cu.free = [t]
            t = causal_conv(y.buf, a.buf, [col("b_conv_w", 8 * j + i) for j in range(3)], [t, cols_token], free=y.free)
            a.free = [t]
            t = DVE.tt(y.buf, y.buf, cb.buf, ALU.mult, after=[t, t_cb])
            cb.free = [t]
            t_hi, t_lo = split_into(c_hi, c_lo, i, y.buf, [t], phase_start if i == 0 else ())
            y.free = [t_hi, t_lo]
            c_ready[i] = t_lo
        m_ready = [None] * 8
        for i in range(8):
            ga, t_a = fm_product("b_ga", i)
            yc, t_y = fm_product("b_out_conv", i, src_hi=c_hi, src_lo=c_lo, ready=c_ready)
            a = temps.next()
            t = SC.act(a.buf, ga.buf, ACT.Sigmoid, after=[t_a, *a.free])
            ga.free = [t]
            m_ready[i] = DVE.tt(merged[:, i, :], a.buf, yc.buf, ALU.mult, after=[t, t_y, *phase_start])
            yc.free = [m_ready[i]]
            a.free = [m_ready[i]]

        phase_start = barrier()
        o_all = at("gla_o", 16 * KB, [P, 8, T])
        v_tm = at("gla_v_tm", 32 * KB, [P, 4, T])
        b_all = at("gla_b", 40 * KB, [P, 4, T])
        gup = at("gate_up", 48 * KB, [16, T])
        glr = at("g_lr", 50 * KB, [16, T])
        q_sb = Ring([at("gla_q", 50 * KB, [P, T])])
        k_sb = Ring([at("gla_k", 52 * KB, [P, T])], phase_start)
        r_sb = Ring([at(f"gla_r{i}", (54 + 2 * i) * KB, [P, T]) for i in range(4)], phase_start)
        gated = Gated("gla", 62 * KB, 256, 64, phase_start)
        SP.do(lambda e: e.dma_start(gup[:, :], dram["gate_w_up"]), phase_start, dma_sem=gup_landed)
        bank, t = fm_product("b_glr", 0)
        t_glr = SC.act(glr[:, :], bank.buf[0:16, :], ACT.Copy, after=[t, *phase_start])
        bank.free = [t_glr]
        b_ready = [None] * 4
        for h in range(4):
            bank = S.next()
            t = PE.mm(bank.buf, gup[:, h * P:(h + 1) * P], glr[:, :], True, True,
                      after=[t_glr, (gup_landed, 16), *bank.free], signal=True)
            zb = b_all[:, h, :]
            s = gated.sq.next()
            t = DVE.ts(zb, bank.buf, col("gate_b", h), None, ALU.add, after=[t, cols_token, *phase_start])
            bank.free = [t]
            t1 = SC.act(s.buf[:, :], zb, ACT.Abs, after=[t, *s.free])
            t1 = SC.act(s.buf[:, :], s.buf[:, :], ACT.Exp, scale=-1.0, after=[t1])
            t1 = SC.act(s.buf[:, :], s.buf[:, :], ACT.Ln, bias=ones[:, 0:1], after=[t1])
            t = DVE.stt(s.buf[:, :], zb, 0.0, s.buf[:, :], ALU.min, ALU.subtract, after=[t1])
            t = DVE.ts(s.buf[:, :], s.buf[:, :], 1.0 / 16.0, None, ALU.mult, after=[t])
            b_ready[h] = gated.running_sum(zb, s.buf[:, :], [t])
            s.free = [b_ready[h]]
            q_sb.slots[0].free = [DVE.last]
        v_done, v_free = [None], list(phase_start)
        o_ready = [None] * 8

        def gla_output(n, h, d):
            o, t = gated.output(n, d, v_tm, v_done[0], h % 2 * 256)
            v_free[:] = [t]
            t = SC.act(o_all[:, 2 * h + d, :], o.buf, ACT.Copy, after=[t, *phase_start])
            o.free = [t]
            sq = gated.sq.next()
            n.sq.append(sq)
            n.t_sq.append(SC.act(sq.buf[:, :], o_all[:, 2 * h + d, :], ACT.Square, after=[t, *sq.free]))

        def finish_gla(n, h):
            for d in range(2):
                gla_output(n, h, d)

        def gla_norm(n, h):
            bank, r = S.next(), gated.rstd.next()
            PE.mm(bank.buf, gated.mean[:, :], n.sq[0].buf[:, :], True, False, after=[n.t_sq[0], gated.const, *bank.free])
            t = PE.mm(bank.buf, gated.mean[:, :], n.sq[1].buf[:, :], False, True, after=[n.t_sq[1]], signal=True)
            n.sq[0].free = n.sq[1].free = [t]
            t_r = inverse_rms(r.buf[:, :], bank, t, after=r.free)
            for i in range(2):
                o = o_all[:, 2 * h + i, :]
                t = DVE.stt(o, o, col("gla_norm", 2 * h + i), r.buf[:, :], ALU.mult, ALU.mult,
                            after=[t_r, n.t_sq[i], cols_token])
                o_ready[2 * h + i] = DVE.tt(o, o, n.r[i].buf[:, :], ALU.mult, after=[t, n.t_r[i]])
                n.r[i].free = [o_ready[2 * h + i]]
            r.free = [t]

        older = last = None
        for h in range(6):
            n = None
            if h in (0, 2):
                if last is not None:
                    gated.scores(last)
                    gated.states(last, v_tm, v_done[0], (h - 1) % 2 * 256)
                    gla_norm(older, h - 2)
                    finish_gla(last, h - 1)
                    older = None
                    last.done = True

                def put(tok, bank, t):
                    v_done[0] = SC.act(v_tm[:, tok, :], bank.buf, ACT.Copy, after=[t, *v_free])
                    bank.free = [v_done[0]]
                tm_product("b_v", h // 2, put)
            if h < 4:
                bank, t = fm_product("b_k", h)
                k = k_sb.next()
                t_k = SC.act(k.buf[:, :], bank.buf, ACT.Copy, after=[t, *k.free])
                bank.free = [t_k]
                n = gated.exponents(b_all[:, h, :], b_ready[h])
                gated.exponentials(n)
                n.r, n.t_r, n.sq, n.t_sq, n.done = [], [], [], [], False
            if older is not None:
                gla_norm(older, h - 2)
            busy = last is not None and not last.done
            v0 = (h - 1) % 2 * 256
            if busy:
                gated.scores(last)
            if n is not None:
                bank, t = fm_product("b_q", h)
                q = q_sb.next()
                t_q = SC.act(q.buf[:, :], bank.buf, ACT.Copy, scale=float(P) ** -0.5, after=[t, *q.free])
                bank.free = [t_q]
            if busy:
                gated.states(last, v_tm, v_done[0], v0)
            if n is not None:
                gated.weigh(n, q.buf[:, :], t_q, k.buf[:, :], t_k)
                q.free = k.free = n.inputs_read
            for i in range(2):
                if n is not None:
                    bank, t = fm_product("b_r", 2 * h + i)
                    s = r_sb.next()
                    t1 = SC.act(s.buf[:, :], bank.buf, ACT.Sigmoid, after=[t, *s.free])
                    t1 = DVE.tt(s.buf[:, :], s.buf[:, :], bank.buf, ALU.mult, after=[t, t1])
                    bank.free = [t1]
                    n.r.append(s)
                    n.t_r.append(t1)
                if busy:
                    gla_output(last, h - 1, i)
            older, last = last, n

        phase_start = barrier()
        g_hi = at("gla_g_hi", 32 * KB, [P, 8, T], F32R)
        g_lo = at("gla_g_lo", 48 * KB, [P, 8, T], F32R)
        m_hi = at("merged_hi", 64 * KB, [P, 8, T], F32R)
        m_lo = at("merged_lo", 80 * KB, [P, 8, T], F32R)
        temps = Ring([at("gb_sb0", 96 * KB, [P, T])[:, :], o_all[:, 0, :]], phase_start)
        g_ready = [split_into(g_hi, g_lo, i, o_all[:, i, :], [o_ready[i]], phase_start if i == 0 else ())[1] for i in range(8)]
        temps.slots[1].free = [g_ready[0]]
        mm_ready = [None] * 8
        for i in range(8):
            gb, t_b = fm_product("b_gb", i)
            yg, t_y = fm_product("b_out_gla", i, src_hi=g_hi, src_lo=g_lo, ready=g_ready)
            s = temps.next()
            t = SC.act(s.buf, gb.buf, ACT.Sigmoid, after=[t_b, *s.free])
            gb.free = [t]
            t = DVE.tt(s.buf, s.buf, yg.buf, ALU.mult, after=[t, t_y])
            yg.free = [t]
            t = DVE.tt(s.buf, s.buf, merged[:, i, :], ALU.add, after=[t, m_ready[i]])
            t_hi, t_lo = split_into(m_hi, m_lo, i, s.buf, [t], ())
            s.free = [t_hi, t_lo]
            mm_ready[i] = t_lo
        for n in range(KT):
            bank, t = fm_product("b_o", n, src_hi=m_hi, src_lo=m_lo, ready=mm_ready,
                                 midway=(start_rms if n == KT - 1 else None))
            residual(n, bank, t, 1.0)
        norm_to_h("b_norm_ffn2")
        ffn("bup2", "bdown2", lambda n: 0.5)

        t_r = finish_rms()
        for k in range(KT):
            t = DVE.stt(x[:, k, :], x[:, k, :], col("b_final_norm", k), rstd, ALU.mult, ALU.mult,
                        after=[t_r, x_ready[k], cols_token])
            SP.do(lambda e, k=k: e.dma_start(dram["out"][:, k, :], x[:, k, :]), [t], dma_sem=out_stored)
        SP.do(lambda e: e.wait_ge(out_stored, 16 * KT), signal=False)
        assert max(ends) <= nc.sbuf_usable_end, (max(ends), nc.sbuf_usable_end, arena)
        assert stream.taken == n_w

        block = ctx.enter_context(nc.Block())

        @block.sync
        def _(eng):
            SP.emit(eng)

        @block.tensor
        def _(eng):
            PE.emit(eng)

        @block.vector
        def _(eng):
            DVE.emit(eng)

        @block.scalar
        def _(eng):
            SC.emit(eng)

        @block.gpsimd
        def _(eng):
            GP.emit(eng)


def _tiles(w, cols=None):
    w = w if cols is None else w[:, cols]
    K, N = w.shape
    return np.ascontiguousarray(w.reshape(K // P, P, N // P, P).transpose(2, 1, 0, 3)).reshape(N // P, P, K)


def _wide(w):
    K, N = w.shape
    return np.ascontiguousarray(w.reshape(4, 2, P, N // T, T).transpose(3, 0, 2, 1, 4)).reshape(N // T, 4, P, 2 * T)


def _vec(v):
    return np.asarray(v).reshape(-1, P).T


def kernel(**inputs):
    import concourse.bacc as _bacc
    from concourse.bass_utils import run_bass_kernel_spmd as _run

    a = {k: np.asarray(v) for k, v in inputs.items()}
    hg, nsa, b_in = a["hg_w_in"][0], a["nsa_w_in"][0], a["w_in_2"][0]
    order = [4 * (2 * (p // 4) + half) + p % 4 for p in range(8) for half in range(2)]
    q_cols = np.concatenate([np.arange(HD * h, HD * h + HD) for h in order])
    v_cols = np.concatenate([np.arange(1792, 2048), np.arange(2304, 2560)])
    kv_cols = np.concatenate([np.arange(1024, 1792), np.arange(2048, 2304)])
    glr = np.zeros((D, P), b_in.dtype)
    glr[:, 0:16] = b_in[:, 5120:5136]
    pe = a["nsa_cmp_pe"][0].reshape(2 * CMP_LEN, HD).T
    parts = {
        "c": _vec(a["c"][0]), "norm_mix0": _vec(a["norm_mix"][0]), "norm_ffn0": _vec(a["norm_ffn"][0]),
        "norm_mix1": _vec(a["norm_mix"][1]), "norm_ffn1": _vec(a["norm_ffn"][1]), "final_norm": _vec(a["final_norm"]),
        "b_norm_ffn1": _vec(a["norm_ffn1_g_2"][0]), "b_norm_mix": _vec(a["norm_mix_g_2"][0]),
        "b_norm_ffn2": _vec(a["norm_ffn2_g_2"][0]), "b_final_norm": _vec(a["final_norm_g_2"]),
        "ada_b": _vec(a["ada_b"].reshape(-1)), "gnorm": _vec(a["hg_gnorm"][0]), "hg_lb": _vec(a["hg_lb"].reshape(-1)),
        "conv_w0": _vec(a["ffn_conv_w"][0].reshape(-1)), "conv_b0": _vec(a["ffn_conv_b"][0]),
        "conv_w1": _vec(a["ffn_conv_w"][1].reshape(-1)), "conv_b1": _vec(a["ffn_conv_b"][1]),
        "b_conv_w": _vec(a["conv_w_2"][0].reshape(-1)), "gate_b": _vec(a["gate_b_2"][0]),
        "gla_norm": _vec(a["gla_norm_g_2"][0]), "pe": np.concatenate([pe, pe], axis=0),
    }
    ada = a["ada_w"].reshape(2, 4, 2, P, 12, T).transpose(0, 4, 1, 3, 2, 5)
    arrays = {
        "cols": np.concatenate([parts[n] for n in COLS], axis=1),
        "x": np.ascontiguousarray(a["x"][0].T.reshape(KT, P, T).transpose(1, 0, 2)),
        "ada": np.ascontiguousarray(ada).reshape(2, 12, 4, P, 2 * T),
        "hg_q": _tiles(hg[:, 0:D]), "hg_f": _tiles(hg[:, D:2 * D]), "hg_v": _wide(hg[:, 2 * D:3 * D]),
        "hg_g": _tiles(hg[:, 3 * D:4 * D]), "hg_out": _tiles(a["hg_w_out"][0]),
        "nsa_q": _tiles(nsa, q_cols), "nsa_kv": _tiles(nsa, kv_cols), "nsa_v": _wide(nsa[:, v_cols]),
        "nsa_gate": np.ascontiguousarray(nsa[:, 2560:2608].reshape(8, P, 48).transpose(1, 0, 2)).reshape(1, P, 8 * 48),
        "nsa_out": _tiles(a["nsa_w_out"][0][q_cols, :]),
        "cmp_w1": np.ascontiguousarray(a["nsa_cmp_w1"][0].reshape(2, CMP_LEN, HD, HD).transpose(2, 0, 1, 3)),
        "cmp_w2": np.ascontiguousarray(a["nsa_cmp_w2"][0].transpose(1, 0, 2)),
        "up0": _tiles(a["ffn_w_up"][0]), "down0": _tiles(a["ffn_w_down"][0]),
        "up1": _tiles(a["ffn_w_up"][1]), "down1": _tiles(a["ffn_w_down"][1]),
        "bup1": _tiles(a["ffn1_w_gu_2"][0]), "bdown1": _tiles(a["ffn1_w_down_2"][0]),
        "bup2": _tiles(a["ffn2_w_gu_2"][0]), "bdown2": _tiles(a["ffn2_w_down_2"][0]),
        "b_conv": _tiles(b_in[:, 0:3 * D]), "b_q": _tiles(b_in[:, 3072:3584]), "b_k": _tiles(b_in[:, 3584:4096]),
        "b_v": _wide(b_in[:, 4096:5120]), "b_glr": _tiles(glr), "b_r": _tiles(b_in[:, 5136:6160]),
        "b_ga": _tiles(b_in[:, 6160:7184]), "b_gb": _tiles(b_in[:, 7184:8208]),
        "b_out_conv": _tiles(a["w_out_conv_2"][0]), "b_out_gla": _tiles(a["w_out_gla_2"][0]),
        "b_o": _tiles(a["w_o_2"][0]), "gate_w_up": a["gate_w_up_2"][0],
    }
    nc = _bacc.Bacc("TRN2", target_bir_lowering=False, num_devices=1)
    dram = {n: nc.dram_tensor(f"in_{n}", v.shape, mybir.dt.from_np(v.dtype), kind="ExternalInput").ap()
            for n, v in arrays.items()}
    dram["out"] = nc.dram_tensor("out_t", (P, KT, T), F32, kind="ExternalOutput").ap()
    build(nc, dram)
    r = _run(nc, [{f"in_{n}": np.ascontiguousarray(v) for n, v in arrays.items()}], core_ids=[0])
    out = r.results[0]["out_t"]
    return np.ascontiguousarray(out.transpose(2, 1, 0)).reshape(1, T, D)
```
